# Optimizing a Trainium2 kernel written in Bass

```python
import jax, jax.numpy as jnp
from jax import lax
import numpy as np

D_MODEL = 1024
BATCH = 1
SEQ = 1024
DEPTH = 2
DEC_BATCH = 8
DEC_SEQ = 4
PAST_LEN = 4096
PAGE_SIZE = 128

N_MIXERS = 2
N_POOL_LAYERS = (DEPTH + 1) // 2
N_ATTN_LAYERS = DEPTH // 2
POOL_EXPAND = 2
POOL_WIDTH = POOL_EXPAND * D_MODEL
POOL_WINDOWS = (2, 4, 8, 16)
N_POOL_GROUPS = len(POOL_WINDOWS)
POOL_GROUP = POOL_WIDTH // N_POOL_GROUPS
POOL_CTX = max(POOL_WINDOWS) - 1
HEAD_DIM = 64
N_HEADS = D_MODEL // HEAD_DIM
ATTN_WIDTH = N_HEADS * HEAD_DIM
Q_BLOCK = 128
FORGET_BIAS_MIN = 1.0
FORGET_BIAS_MAX = 10.0
RMS_EPS = 1e-6
F32 = jnp.float32

kernel_name = "pool_fox_hybrid_step"

def rms_norm(x, g):
    xf = x.astype(F32)
    y = xf * lax.rsqrt(jnp.mean(xf * xf, axis=-1, keepdims=True) + RMS_EPS)
    return (y * g.astype(F32)).astype(x.dtype)

def pool_mixer(h, prefix, start, w_in, mix, scale, w_out):
    T = h.shape[1]
    uz = h @ w_in
    u, z = jnp.split(uz, 2, axis=-1)
    ext = jnp.concatenate([prefix.astype(u.dtype), u], axis=1)
    cs = jnp.cumsum(ext.astype(F32), axis=1)
    cs = jnp.pad(cs, ((0, 0), (1, 0), (0, 0)))
    pos = start + jnp.arange(T, dtype=jnp.int32)
    u32 = u.astype(F32)
    outs = []
    for g, w in enumerate(POOL_WINDOWS):
        sl = slice(g * POOL_GROUP, (g + 1) * POOL_GROUP)
        hi = cs[:, POOL_CTX + 1:POOL_CTX + 1 + T, sl]
        lo = cs[:, POOL_CTX + 1 - w:POOL_CTX + 1 - w + T, sl]
        cnt = jnp.minimum(pos + 1, w).astype(F32)[None, :, None]
        pooled = (hi - lo) / cnt - u32[..., sl]
        outs.append(jnp.einsum('btc,cd->btd', pooled, mix[g].astype(F32)))
    y = jnp.concatenate(outs, axis=-1) * scale.astype(F32)
    y = (y * jax.nn.silu(z.astype(F32))).astype(h.dtype)
    return y @ w_out, ext[:, -POOL_CTX:]

def fox_project(h, w_in, b_f):
    B, T, _ = h.shape
    proj = h @ w_in
    q, k, v, z, f = jnp.split(proj, [ATTN_WIDTH, 2 * ATTN_WIDTH, 3 * ATTN_WIDTH, 4 * ATTN_WIDTH], axis=-1)
    shp = (B, T, N_HEADS, HEAD_DIM)
    logf = jax.nn.log_sigmoid(f.astype(F32) + b_f.astype(F32))
    return q.reshape(shp), k.reshape(shp), v.reshape(shp), z, logf

def fox_attend(q, cq, qpos, k, ck, kpos, v):
    B, T = q.shape[:2]
    blk = Q_BLOCK if T % Q_BLOCK == 0 else T
    nb = T // blk
    scale = HEAD_DIM ** -0.5
    ckT = jnp.swapaxes(ck, 1, 2)

    def one(args):
        qb, cqb, qpb = args
        s = jnp.einsum('bqhd,bkhd->bhqk', qb, k, preferred_element_type=F32) * scale
        s = s + jnp.swapaxes(cqb, 1, 2)[..., :, None] - ckT[:, :, None, :]
        s = jnp.where((kpos[None, :] <= qpb[:, None])[None, None], s, -jnp.inf)
        p = jax.nn.softmax(s, axis=-1)
        return jnp.einsum('bhqk,bkhd->bqhd', p.astype(v.dtype), v)

    qs = q.reshape(B, nb, blk, N_HEADS, HEAD_DIM).transpose(1, 0, 2, 3, 4)
    cqs = cq.reshape(B, nb, blk, N_HEADS).transpose(1, 0, 2, 3)
    qps = qpos.reshape(nb, blk)
    o = lax.map(one, (qs, cqs, qps))
    return o.transpose(1, 0, 2, 3, 4).reshape(B, T, ATTN_WIDTH)

def fox_prompt(h, w_in, b_f, w_out):
    T = h.shape[1]
    q, k, v, z, logf = fox_project(h, w_in, b_f)
    c = jnp.cumsum(logf, axis=1)
    pos = jnp.arange(T, dtype=jnp.int32)
    o = fox_attend(q, c, pos, k, c, pos, v)
    y = (o * jax.nn.silu(z)).astype(h.dtype) @ w_out
    return y, k, v, logf

def fox_sample(h, ck_pool, cv_pool, cl_pool, page_table, w_in, b_f, w_out):
    B, T, _ = h.shape
    P = page_table.shape[1] * ck_pool.shape[1]
    q, k, v, z, logf = fox_project(h, w_in, b_f)
    kp = ck_pool[page_table].reshape(B, P, N_HEADS, HEAD_DIM).astype(k.dtype)
    vp = cv_pool[page_table].reshape(B, P, N_HEADS, HEAD_DIM).astype(v.dtype)
    lp = cl_pool[page_table].reshape(B, P, N_HEADS).astype(F32)
    c_past = lp - lax.cumsum(lp, axis=1, reverse=True)
    c_new = jnp.cumsum(logf, axis=1)
    k_all = jnp.concatenate([kp, k], axis=1)
    v_all = jnp.concatenate([vp, v], axis=1)
    c_all = jnp.concatenate([c_past, c_new], axis=1)
    kpos = jnp.arange(P + T, dtype=jnp.int32)
    qpos = P + jnp.arange(T, dtype=jnp.int32)
    o = fox_attend(q, c_new, qpos, k_all, c_all, kpos, v_all)
    y = (o * jax.nn.silu(z)).astype(h.dtype) @ w_out
    return y, k, v, logf

def setup_inputs(seed: int = 0) -> dict:
    key = jax.random.key(seed)
    ks = jax.random.split(key, 20)
    nrm = jax.random.normal
    n_pages = PAST_LEN // PAGE_SIZE
    n_used = DEC_BATCH * n_pages
    n_phys = n_used + max(1, n_used // 4)
    page_table = jax.random.permutation(ks[0], n_phys)[:n_used].reshape(DEC_BATCH, n_pages).astype(jnp.int32)
    head_bias = jnp.linspace(FORGET_BIAS_MIN, FORGET_BIAS_MAX, N_HEADS, dtype=F32)
    return {
        "x_prompt": nrm(ks[1], (BATCH, SEQ, D_MODEL), F32),
        "x_sample": nrm(ks[2], (DEC_BATCH, DEC_SEQ, D_MODEL), F32),
        "state_pool": nrm(ks[3], (N_POOL_LAYERS, DEC_BATCH, POOL_CTX, POOL_WIDTH), F32),
        "cache_k": nrm(ks[4], (N_ATTN_LAYERS, n_phys, PAGE_SIZE, N_HEADS, HEAD_DIM), F32),
        "cache_v": nrm(ks[5], (N_ATTN_LAYERS, n_phys, PAGE_SIZE, N_HEADS, HEAD_DIM), F32),
        "cache_logf": jax.nn.log_sigmoid(head_bias + 0.5 * nrm(ks[6], (N_ATTN_LAYERS, n_phys, PAGE_SIZE, N_HEADS), F32)),
        "page_table": page_table,
        "norm_g": 1.0 + 0.02 * nrm(ks[7], (DEPTH, D_MODEL), F32),
        "w_in_pool": nrm(ks[8], (N_POOL_LAYERS, D_MODEL, 2 * POOL_WIDTH), F32) * D_MODEL ** -0.5,
        "pool_mix": nrm(ks[9], (N_POOL_LAYERS, N_POOL_GROUPS, POOL_GROUP, POOL_GROUP), F32) * POOL_GROUP ** -0.5,
        "pool_scale": 1.0 + 0.1 * nrm(ks[10], (N_POOL_LAYERS, POOL_WIDTH), F32),
        "w_out_pool": nrm(ks[11], (N_POOL_LAYERS, POOL_WIDTH, D_MODEL), F32) * POOL_WIDTH ** -0.5,
        "w_in_attn": nrm(ks[12], (N_ATTN_LAYERS, D_MODEL, 4 * ATTN_WIDTH + N_HEADS), F32) * D_MODEL ** -0.5,
        "b_forget": head_bias + 0.1 * nrm(ks[13], (N_ATTN_LAYERS, N_HEADS), F32),
        "w_out_attn": nrm(ks[14], (N_ATTN_LAYERS, ATTN_WIDTH, D_MODEL), F32) * ATTN_WIDTH ** -0.5,
        "final_norm": 1.0 + 0.02 * nrm(ks[15], (D_MODEL,), F32),
    }

def reference(x_prompt, x_sample, state_pool, cache_k, cache_v, cache_logf, page_table,
              norm_g, w_in_pool, pool_mix, pool_scale, w_out_pool,
              w_in_attn, b_forget, w_out_attn, final_norm):
    P = page_table.shape[1] * cache_k.shape[2]
    xp, xs = x_prompt, x_sample
    pool_p, pool_s = [], []
    kp_l, vp_l, lp_l, ks_l, vs_l, ls_l = [], [], [], [], [], []
    for i in range(DEPTH):
        j = i // N_MIXERS
        hp = rms_norm(xp, norm_g[i])
        hs = rms_norm(xs, norm_g[i])
        if i % N_MIXERS == 0:
            zero_prefix = jnp.zeros((hp.shape[0], POOL_CTX, POOL_WIDTH), hp.dtype)
            yp, sp = pool_mixer(hp, zero_prefix, 0, w_in_pool[j], pool_mix[j], pool_scale[j], w_out_pool[j])
            ys, ss = pool_mixer(hs, state_pool[j], P, w_in_pool[j], pool_mix[j], pool_scale[j], w_out_pool[j])
            pool_p.append(sp)
            pool_s.append(ss)
        else:
            yp, kp, vp, lp = fox_prompt(hp, w_in_attn[j], b_forget[j], w_out_attn[j])
            ys, kn, vn, ln = fox_sample(hs, cache_k[j], cache_v[j], cache_logf[j], page_table,
                                        w_in_attn[j], b_forget[j], w_out_attn[j])
            kp_l.append(kp); vp_l.append(vp); lp_l.append(lp)
            ks_l.append(kn); vs_l.append(vn); ls_l.append(ln)
        xp = xp + yp
        xs = xs + ys
    y_prompt = rms_norm(xp, final_norm)
    y_sample = rms_norm(xs, final_norm)
    return (y_prompt, y_sample, jnp.stack(pool_p), jnp.stack(pool_s),
            jnp.stack(kp_l), jnp.stack(vp_l), jnp.stack(lp_l),
            jnp.stack(ks_l), jnp.stack(vs_l), jnp.stack(ls_l))


_drawn_inputs = setup_inputs


def setup_inputs(seed=0):
    import zlib

    import numpy as np

    out = dict(_drawn_inputs(seed))
    spreads = {}
    factors = {}
    for name, (base, spread) in spreads.items():
        noise = np.random.default_rng([zlib.crc32(name.encode()), seed]).standard_normal(out[name].shape)
        drawn = base * np.exp(spread * noise) if base else spread * noise
        out[name] = __import__('jax').numpy.asarray(drawn.astype(out[name].dtype))
    for name, factor in factors.items():
        out[name] = (out[name] * factor).astype(out[name].dtype)
    return out
```

```python
from contextlib import ExitStack

import numpy as np

import concourse.bass as bass
from concourse import mybir

F32 = mybir.dt.float32
F32R = mybir.dt.float32r
BF16 = mybir.dt.bfloat16
I32 = mybir.dt.int32
ALU = mybir.AluOpType
ACT = mybir.ActivationFunctionType
AX = mybir.AxisListType.X

P = 128
DM = 1024
SEQ = 1024
NB, NQ = 8, 4
TS = NB * NQ
PW = 2048
WINDOWS = (2, 4, 8, 16)
NG = len(WINDOWS)
CTX = 15
NH, HD = 16, 64
PAGES, PAGE = 32, 128
PAST = PAGES * PAGE
KT8 = DM // P
TT = SEQ // P
EPS = 1e-6
NEG = -1e30
AUG = HD + 2
QSCALE = HD ** -0.5

PAD = 16
SEG = CTX + NQ
U_S = PAD + SEQ
UW = U_S + NB * SEG
GC = CTX + TS

C_ID, C_SUM4, C_SEL = 0, 128, 160
C_MQ, C_NEG, C_TRI = 288, 544, 800
C_CAUS, C_INV, C_HM = 928, 1056, 1072
C_END = 1076

QBLOCKS = (0, 7, 1, 6, 2, 5, 3, 4)


def constants():
    c = np.zeros((P, C_END), np.float32)
    r = np.arange(P)
    c[:, C_ID:C_ID + P] = np.eye(P)
    c[r, C_SUM4 + r % TS] = 1.0
    head = np.where(r % 32 < 16, 4 * (r // 32) + (r % 32) // 4, -1)
    for h in range(NH):
        c[h, C_SEL:C_SEL + P] = head == h
    tok = np.arange(TS)[None]
    for b in range(NB):
        last = (NQ * b + r % NQ)[:, None]
        c[:, C_MQ + TS * b:C_MQ + TS * (b + 1)] = tok == last
        seen = (tok >= NQ * b) & (tok <= last)
        c[:, C_NEG + TS * b:C_NEG + TS * (b + 1)] = np.where(seen, 0.0, NEG)
    c[:, C_TRI:C_TRI + P] = (r[:, None] > r[None]) & (r[:, None] // PAGES == r[None] // PAGES)
    c[:, C_CAUS:C_CAUS + P] = np.where(r[None] > r[:, None], NEG, 0.0)
    c[:, C_INV:C_INV + 16] = 1.0 / np.arange(1, 17, dtype=np.float32)
    for hh in range(4):
        c[:, C_HM + hh] = (r % 32) // 4 == hh
    return c


CHUNKS = [("u", 0), ("u", 1), ("u", 2), ("u", 3), ("z", 0), ("m", 0), ("z", 1), ("m", 1), ("z", 2),
          ("o", 0), ("o", 1), ("m", 2), ("z", 3), ("m", 3), ("o", 2), ("o", 3)]
NCH = len(CHUNKS)
C_L0 = NG * NCH
CR_W = 2
B7 = 14
B7_AT = {("st", 0): 0, ("u", 0): 1, ("u", 1): 2, ("u", 2): 3, ("u", 3): 4, ("g", 0): 5, ("z", 0): 6,
         ("m", 0): 7, ("z", 1): 8, ("m", 1): 9, ("z", 2): 10, ("m", 2): 11, ("z", 3): 12, ("m", 3): 13}


def before(kinds, n):
    return sum(CHUNKS[i][0] in kinds for i in range(n))


def build(nc, x_prompt, x_sample, state_pool, cache_k, cache_v, cache_logf, page_table, norm_g,
          w_in_pool, pool_mix, pool_scale, w_out_pool, w_in_attn, b_forget, w_out_attn, final_norm,
          consts, y_prompt, y_sample, pool_prompt, pool_sample, k_prompt, v_prompt, logf_prompt,
          k_sample, v_sample, logf_sample):
    n_phys = cache_k.shape[1]

    def internal(name, shape):
        return nc.dram_tensor(name, shape, F32, kind="Internal").ap()

    q_aug = internal("q_aug", (NH, AUG, SEQ))
    k_aug = internal("k_aug", (NH, AUG, SEQ))
    decay = internal("decay", (NB, NH, PAST))
    o_smp = internal("o_smp", (TS, DM))
    x1_scr = internal("x1_scr", (SEQ, DM))

    with ExitStack() as ctx:
        base = (nc.sbuf_base + 63) // 64 * 64
        at = [base]

        def place(name, shape, dt=F32, where=None):
            n = int(np.prod(shape[1:])) * (2 if dt == BF16 else 4)
            off = at[0] if where is None else where
            if where is None:
                at[0] = off + (n + 31) // 32 * 32
            return nc.alloc_sbuf_tensor_at(name, list(shape), dt, offset=off)

        def sem(name):
            return ctx.enter_context(nc.semaphore(name))

        con = place("con", [P, C_END])
        ident = con[:, C_ID:C_ID + P]
        sum4 = con[:, C_SUM4:C_SUM4 + TS]
        ident_b = place("ident_b", [P, P], BF16)
        caus_b = place("caus_b", [P, P], BF16)
        x_s = place("x_s", [64, DM])
        q_s = place("q_s", [P, KT8, TS])
        k_s = place("k_s", [P, KT8, TS])
        q_bd = place("q_bd", [P, KT8, 32])
        d_new = place("d_new", [P, NB, TS])
        cq = place("cq", [P, NB])
        ss = place("ss", [P, TT + 1])
        st_max = place("st_max", [P, 9])
        st_nm = place("st_nm", [P, 1])
        st_sum = place("st_sum", [P, 9])
        st_l = place("st_l", [P, 2])
        hm_l = place("hm_l", [P, 4])
        pp_nm = place("pp_nm", [P, 2])
        pp_l = place("pp_l", [P, 2])
        pp_r = place("pp_r", [P, 2])
        pt_sb = place("pt_sb", [1, NB * PAGES], I32)
        g_t = place("g_t", [P, 2, KT8])
        sc_t = place("sc_t", [P, PW // P])
        bf_t = place("bf_t", [NH, 1])
        h_s = place("h_s", [P, KT8, TS])
        at_in = at[0]
        st_in = place("st_in", [NB * CTX, 512])
        st_t = place("st_t", [P, 4, NB * CTX])
        g_in = place("g_in", [P, 4, GC])
        g_out = place("g_out", [GC, 512])
        p_s = place("p_s", [P, 4, TS])
        ym_s = place("ym_s", [P, TS])
        sz_s = place("sz_s", [P, TS])
        y_s = place("y_s", [P, 2, TS])
        at_px = at[0]
        px_sb = place("px_sb", [P, P])
        ks_st = place("ks_st", [P, TS])
        vs_st = place("vs_st", [P, TS])
        ones = place("ones", [P, P])
        idx = place("idx", [P, 2], I32)
        cr_sb = place("cr_sb", [P, TS])
        big = at[0]

        def big_at(n):
            return big + 4 * n

        h_hi = place("h_hi", [P, KT8, SEQ], F32R, big_at(0))
        h_lo = place("h_lo", [P, KT8, SEQ], F32R, big_at(8192))
        w_raw = [place(f"w_raw{i}", [P, 1024], F32, big_at(16384 + 1024 * i)) for i in range(2)]
        w_hi = [place(f"w_hi{i}", [P, 1024], F32R, big_at(18432 + 1024 * i)) for i in range(2)]
        w_lo = [place(f"w_lo{i}", [P, 1024], F32R, big_at(20480 + 1024 * i)) for i in range(2)]
        AT_PO, AT_Y, AT_U = 22528, 30720, 34816
        po_hi = place("po_hi", [P, 4, SEQ], F32R, big_at(AT_PO))
        po_lo = place("po_lo", [P, 4, SEQ], F32R, big_at(AT_PO + 4096))
        y_hi = place("y_hi", [P, 2, SEQ], F32R, big_at(AT_Y))
        y_lo = place("y_lo", [P, 2, SEQ], F32R, big_at(AT_Y + 2048))
        u_sb = place("u_sb", [P, UW], F32, big_at(AT_U))
        t1 = place("t1", [P, UW], F32, big_at(AT_U + UW))
        t2 = place("t2", [P, UW], F32, big_at(AT_U + 2 * UW))
        AT_X = AT_U + 3 * UW + 48
        x_p = place("x_p", [P, TT, DM], F32, big_at(AT_X))
        xn = place("xn", [P, TT, DM], F32, big_at(AT_PO))
        xn_s = place("xn_s", [TS, DM], F32, big_at(AT_Y))
        xt_s = place("xt_s", [TS, DM], F32, big_at(AT_Y + 1024))
        junk = place("junk", [P, DM], F32, big_at(AT_Y + 2048))
        q_st = place("q_st", [P, SEQ], F32, big_at(AT_PO))
        k_st = place("k_st", [P, SEQ], F32, big_at(AT_PO + 1024))
        v_st = place("v_st", [P, SEQ], F32, big_at(AT_PO + 2048))
        k_tm = place("k_tm", [P, TT, P], F32, big_at(AT_PO + 3072))
        v_tm = place("v_tm", [P, TT, P], F32, big_at(AT_PO + 4096))
        ks_tm = place("ks_tm", [TS, DM], F32, big_at(AT_PO + 5120))
        wf = place("wf", [P, KT8, P], F32, big_at(AT_Y + 3072))
        LW = SEQ + TS
        lf = [place(f"lf{i}", [NH, LW], F32, big_at(AT_PO + 6400 if i == 0 else AT_Y + LW * (i - 1)))
              for i in range(5)]
        lp = place("lp", [P, 2048], F32, big_at(AT_Y))
        pfx = [place(f"pfx{i}", [P, NH, PAGE], F32, big_at(AT_Y + 2048 * (i + 1))) for i in range(2)]
        tot = place("tot", [P, 2, NH], F32, big_at(AT_Y + 6144))
        lf_tm = place("lf_tm", [P, TT, NH], F32, big_at(AT_Y + 6176))
        lfs_tm = place("lfs_tm", [TS, NH], F32, big_at(AT_Y + 6304))
        c_s = place("c_s", [NH, TS], F32, big_at(AT_Y + 6320))
        mq_w = place("mq_w", [P, NB, TS], F32, big_at(AT_Y + 6352))
        z_t = place("z_t", [P, KT8, SEQ + TS], F32, big_at(AT_X))
        vs_tm = place("vs_tm", [TS, DM], F32, big_at(37408))
        o_raw = place("o_raw", [P, 4, HD], F32, at_in)
        o_n = place("o_n", [P, HD], F32, at_in + 1024)
        KR, VR = 8, 8
        k_pg = place("k_pg", [P, KR, DM], F32, big_at(0))
        v_pg = place("v_pg", [P, VR, DM], F32, big_at(8192))
        kt = [place(f"kt{i}", [P, KT8, 256], F32, big_at(16384 + 2048 * i)) for i in range(2)]
        s_sb = place("s_sb", [P, PAST + TS], F32, big_at(20480))
        d_sb = place("d_sb", [P, PAST], F32, big_at(24608))
        pt_s = place("pt_s", [P, 4, P], F32, big_at(28704))
        qa = place("qa", [AUG, 2, SEQ], F32, big_at(29216))
        ka = place("ka", [AUG, 2, SEQ], F32, big_at(31264))
        v_pr = place("v_pr", [P, TT, P], F32, big_at(33312))
        p_p = place("p_p", [P, 2, SEQ], F32, big_at(34336))
        pt_p = place("pt_p", [P, TT, P], F32, big_at(36384))
        w_o = place("w_o", [P, KT8, DM], F32, big_at(0))
        x1_t = [place(f"x1_t{i}", [P, DM], F32, big_at(16384 + 1024 * i)) for i in range(3)]
        fn_b = place("fn_b", [P, DM], F32, big_at(29216))
        jk2 = place("jk2", [P, DM], F32, big_at(30240))
        os_tm = place("os_tm", [TS, DM], F32, big_at(31264))
        assert big_at(AT_X + KT8 * (SEQ + TS)) <= nc.sbuf_usable_end, (big, nc.sbuf_usable_end)

        ps_a = ctx.enter_context(nc.psum_tensor("ps_a", [P, 1024], F32))
        ps_b = ctx.enter_context(nc.psum_tensor("ps_b", [P, 1024], F32))
        b4, b5, b6, b7 = (ctx.enter_context(nc.psum_tensor(f"b{i}", [P, 512], F32)) for i in range(4, 8))
        out_b = (b4, b5)

        ld_small, ld_x, ld_wf, ld_st = sem("ld_small"), sem("ld_x"), sem("ld_wf"), sem("ld_st")
        ld_w = [sem("ld_w0"), sem("ld_w1")]
        ld_lp = [sem("ld_lp0"), sem("ld_lp1")]
        spill, st_pool, st_aug, st_tm, st_lf, st_dec, st_dense = (
            sem(n) for n in ("spill", "st_pool", "st_aug", "st_tm", "st_lf", "st_dec", "st_dense"))
        pool_free, go_free, pool_held = sem("pool_free"), sem("go_free"), sem("pool_held")
        smp_used, tile_done, pe_b7, pe_o = sem("smp_used"), sem("tile_done"), sem("pe_b7"), sem("pe_o")
        pe_nt, pe_nts, pe_tm, pe_tail = sem("pe_nt"), sem("pe_nts"), sem("pe_tm"), sem("pe_tail")
        act_hi, act_px, act_b7, act_u, act_z = (sem(n) for n in ("act_hi", "act_px", "act_b7", "act_u", "act_z"))
        act_ss, act_sq, act_nt, act_t, act_lf = (sem(n) for n in ("act_ss", "act_sq", "act_nt", "act_t", "act_lf"))
        dve_c, dve_lo, dve_px, dve_pool = sem("dve_c"), sem("dve_lo"), sem("dve_px"), sem("dve_pool")
        dve_m, dve_mf, dve_o, dve_xt = sem("dve_m"), sem("dve_mf"), sem("dve_o"), sem("dve_xt")
        dve_var, dve_xn, dve_nt, dve_nts = sem("dve_var"), sem("dve_xn"), sem("dve_nt"), sem("dve_nts")
        dve_dec = sem("dve_dec")
        dve_lf, dve_tm, dve_tot, dve_tail = sem("dve_lf"), sem("dve_tm"), sem("dve_tot"), sem("dve_tail")
        dve_cst, dve_wf = sem("dve_cst"), sem("dve_wf")

        PX_L0, B7_L0 = NG * 12, NG * B7
        N_SMALL = 16 * 6


        def tile_ps(parity):
            return ps_b if parity else ps_a

        dense = nc.Block()
        block = dense.__enter__()

        @block.sync
        def _(sp):
            sp.dma_start(x_p[:, 0:4, :], x_prompt[0, 0:512, :].rearrange("(t p) d -> p t d", p=P)).then_inc(ld_x, 16)
            sp.dma_start(x_p[:, 4:8, :], x_prompt[0, 512:1024, :].rearrange("(t p) d -> p t d", p=P)).then_inc(ld_x, 16)
            sp.dma_start(x_s[0:TS, :], x_sample.rearrange("b q d -> (b q) d")).then_inc(ld_x, 16)

            with sp.Fori(0, NG) as g:
                sp.wait_ge(pe_b7, g * B7 + 1)
                sp.dma_start(st_in[:, :], state_pool[0].rearrange("b t c -> (b t) c")[:, bass.ds(g * 512, 512)])\
                  .then_inc(ld_st, 16)
                for n, (kind, i) in enumerate(CHUNKS):
                    sp.wait_ge(dve_lo, g * NCH + n + 1)
                    sp.wait_ge(smp_used, g * NCH + n + 1)
                    dst = w_raw[n % 2]
                    if kind in "uz":
                        col = g * 512 + ((PW if kind == "z" else 0) + 128 * i)
                        sp.dma_start(dst[:, :].rearrange("p (k n) -> p k n", n=P),
                                     w_in_pool[0].rearrange("(k p) c -> p k c", p=P)[:, :, bass.ds(col, P)])\
                          .then_inc(ld_w[n % 2], 16)
                    elif kind == "m":
                        sp.dma_start(dst[:, 0:512].rearrange("p (c n) -> p c n", n=P),
                                     pool_mix[0, bass.ds(g, 1), :, 128 * i:128 * i + 128]
                                     .rearrange("o (c p) n -> p (o c) n", p=P)).then_inc(ld_w[n % 2], 16)
                    else:
                        row = g * 512 + 256 * (i // 2)
                        half = i % 2
                        sp.dma_start(dst[:, :].rearrange("p (k n) -> p k n", n=512),
                                     w_out_pool[0, bass.ds(row, 256), 512 * half:512 * half + 512]
                                     .rearrange("(k p) n -> p k n", p=P)).then_inc(ld_w[n % 2], 16)

            sp.wait_ge(dve_o, 2 + NG * 32)
            sp.dma_start(x1_scr.rearrange("(t p) d -> p t d", p=P), x_p[:, :, :]).then_inc(spill, 16)
            sp.wait_ge(dve_wf, 1)
            sp.dma_start(wf[:, :, 0:NH], w_in_attn[0, :, 4 * DM:4 * DM + NH].rearrange("(k p) n -> p k n", p=P))\
              .then_inc(ld_wf, 16)
            with sp.Fori(0, KT8) as f:
                for n in range(4):
                    sp.wait_ge(dve_lo, f * 4 + (C_L0 + n + 2))
                    sp.wait_ge(smp_used, f * 4 + (C_L0 + n + 2))
                    sp.dma_start(w_raw[n % 2][:, :].rearrange("p (k n) -> p k n", n=P),
                                 w_in_attn[0].rearrange("(k p) c -> p k c", p=P)[:, :, bass.ds(f * P + n * DM, P)])\
                      .then_inc(ld_w[n % 2], 16)
            for t in range(2):
                sp.wait_ge(dve_dec, t + 1)
                for b in range(4):
                    sp.dma_start(decay[4 * t + b].rearrange("h (g k) -> g h k", k=PAGE),
                                 pfx[t][32 * b:32 * b + 32, :, :]).then_inc(st_dec, 16)
            sp.wait_ge(dve_tail, 1)
            sp.dma_start(logf_prompt[0, 0].rearrange("(t p) h -> p t h", p=P), lf_tm[:, :, :]).then_inc(st_dense, 16)
            sp.dma_start(logf_sample[0].rearrange("b q h -> (b q) h"), lfs_tm[:, :]).then_inc(st_dense, 16)
            sp.wait_ge(act_b7, 1 + B7_L0 + 1 + 6 * KT8)
            sp.dma_start(k_sample[0].rearrange("b q h d -> (b q) (h d)"), ks_tm[:, :]).then_inc(st_dense, 16)
            sp.dma_start(v_sample[0].rearrange("b q h d -> (b q) (h d)"), vs_tm[:, :]).then_inc(st_dense, 16)
            sp.wait_ge(st_dense, 64)
            sp.wait_ge(st_dec, 16 * 8)
            sp.wait_ge(spill, 16)

        def hold(pool):
            pool.sem_inc(pool_held, 1)

        @block.gpsimd
        def _(pool):
            pool.sem_inc(go_free, 1)
            pool.sem_inc(pool_free, 1)
            pool.dma_start(pool_sample[0, :, 0:CTX - NQ, :], state_pool[0, :, NQ:CTX, :]).then_inc(st_pool, 16)
            with pool.Fori(0, NG) as g:
                pool.wait_ge(act_b7, g * B7 + (1 + B7_AT["g", 0] + 1))
                hold(pool)
                pool.dma_start(pool_prompt[0, 0, :, bass.ds(g * 512, 512)], g_out[0:CTX, :]).then_inc(st_pool, 16)
                pool.dma_start(pool_sample[0].rearrange("b t c -> b t c")[:, CTX - NQ:CTX, bass.ds(g * 512, 512)],
                               g_out[CTX:GC, :]).then_inc(st_pool, 16)
                pool.wait_ge(st_pool, g * 32 + 48)
                pool.sem_inc(go_free, 1)

            def stores(f):
                pool.wait_ge(act_t, f * 4 + 3)
                hold(pool)
                for hh in range(2):
                    pool.dma_start(q_aug[bass.ds(f * 2 + hh, 1), 0:HD, :].rearrange("o d t -> d (o t)"),
                                   q_st[64 * hh:64 * hh + 64, :]).then_inc(st_aug, 16)
                pool.wait_ge(act_t, f * 4 + 4)
                hold(pool)
                for hh in range(2):
                    pool.dma_start(k_aug[bass.ds(f * 2 + hh, 1), 0:HD, :].rearrange("o d t -> d (o t)"),
                                   k_st[64 * hh:64 * hh + 64, :]).then_inc(st_aug, 16)
                pool.wait_ge(dve_tm, f * 4 + 4)
                hold(pool)
                pool.dma_start(k_prompt[0, 0].rearrange("(t p) h d -> p t (h d)", p=P)[:, :, bass.ds(f * P, P)],
                               k_tm[:, :, :]).then_inc(st_tm, 16)
                pool.wait_ge(dve_tm, f * 4 + 6)
                hold(pool)
                pool.dma_start(v_prompt[0, 0].rearrange("(t p) h d -> p t (h d)", p=P)[:, :, bass.ds(f * P, P)],
                               v_tm[:, :, :]).then_inc(st_tm, 16)
                pool.wait_ge(st_aug, f * 64 + 64)
                pool.wait_ge(st_tm, f * 32 + 32)
                pool.sem_inc(pool_free, 1)

            stores(0)
            pool.wait_ge(dve_lf, 6)
            for dst, src in ((q_aug[:, HD, :], lf[1]), (q_aug[:, HD + 1, :], lf[3]),
                             (k_aug[:, HD, :], lf[3]), (k_aug[:, HD + 1, :], lf[2])):
                pool.dma_start(dst, src[:, 0:SEQ]).then_inc(st_lf, 16)
            pool.wait_ge(st_lf, 64)
            for t, tiles in ((0, (1, 4)), (1, (4, KT8))):
                if t:
                    pool.wait_ge(dve_tot, 1)
                pool.indirect_dma_start(lp[:, :], None, cache_logf[0].rearrange("n k h -> n (k h)"),
                                        bass.IndirectOffsetOnAxis(ap=idx[:, t:t + 1], axis=0)).then_inc(ld_lp[t], 16)
                with pool.Fori(*tiles) as f:
                    stores(f)

        @block.scalar
        def _(act):
            act.dma_start(con[:, :], consts).then_inc(ld_small, 16)
            act.dma_start(g_t[:, :, :], norm_g.rearrange("n (k p) -> p n k", p=P), allow_slow_non_contiguous=True).then_inc(ld_small, 16)
            act.dma_start(sc_t[:, :], pool_scale[0].rearrange("(k p) -> p k", p=P), allow_slow_non_contiguous=True).then_inc(ld_small, 16)
            act.dma_start(bf_t[:, :], b_forget[0].rearrange("(h o) -> h o", o=1)).then_inc(ld_small, 16)
            act.dma_start(pt_sb[:, :], page_table.rearrange("(o b) g -> o (b g)", o=1)).then_inc(ld_small, 16)
            act.dma_start(idx[:, :], page_table.rearrange("(t b) g -> (b g) t", t=2), allow_slow_non_contiguous=True).then_inc(ld_small, 16)
            act.sem_inc(act_px, 1)
            act.sem_inc(act_b7, 1)
            act.sem_inc(act_z, 1)
            act.sem_inc(act_t, 1)
            act.wait_ge(ld_small, N_SMALL)

            def norm(n):
                act.wait_ge(dve_cst, 1)
                if n == 0:
                    act.wait_ge(ld_x, 48)
                else:
                    act.wait_ge(dve_o, 2 + NG * 32)
                for i in range(TT):
                    nc.scalar.activation(xn[:, i, :], x_p[:, i, :], ACT.Square, accum_out=ss[:, i:i + 1])
                act.wait_ge(dve_xt, n + 1)
                nc.scalar.activation(junk[0:TS, :], xt_s[:, :], ACT.Square,
                                     accum_out=ss[0:TS, TT:TT + 1]).then_inc(act_ss, 1)
                act.wait_ge(dve_var, n + 1)
                nc.scalar.activation(ss[:, :], ss[:, :], ACT.Sqrt).then_inc(act_sq, 1)
                for f in range(16):
                    act.wait_ge(pe_nt, 16 * n + f + 1)
                    k, half = f % 8, f // 8
                    nc.scalar.activation(h_hi[:, k, 512 * half:512 * half + 512], out_b[f % 2][:, :], ACT.Copy,
                                         scale=g_t[:, n, k:k + 1]).then_inc(act_nt, 1)

            def hi(c, slot, raw, width=1024):
                act.wait_ge(tile_done, c + 1)
                nc.scalar.copy(w_hi[slot][:, 0:width], raw[:, 0:width]).then_inc(act_hi, 1)

            def px(smp):
                act.wait_ge(smp_used, smp)
                nc.scalar.copy(px_sb[:, :], b6[:, 0:P]).then_inc(act_px, 1)

            def group(g, last):
                act.wait_ge(pe_b7, g * B7 + (B7 + 1))
                nc.scalar.copy(st_t[:, :, :].rearrange("p i r -> p (i r)"), b7[:, 0:480]).then_inc(act_b7, 1)
                for n, (kind, i) in enumerate(CHUNKS):
                    if kind != "o":
                        px(g * NCH + (n + 1 + CR_W))
                    if n < NCH - 1:
                        act.wait_ge(ld_w[(n + 1) % 2], g * (8 * 16) + 16 * ((n + 1) // 2 + 1))
                        hi(g * NCH + (n + 1), (n + 1) % 2, w_raw[(n + 1) % 2], 512 if CHUNKS[n + 1][0] == "m" else 1024)
                    elif not last:
                        act.wait_ge(ld_w[0], g * (8 * 16) + (8 * 16 + 16))
                        hi(g * NCH + NCH, 0, w_raw[0])
                    ps = tile_ps((before("uzm", n)) % 2)
                    b7_at = g * B7 + (B7 + B7_AT.get((kind, i), 0) + 1)
                    if kind == "u":
                        act.wait_ge(tile_done, g * NCH + (n + 1 + CR_W))
                        act.wait_ge(dve_pool, g * 4 + (i + 1))
                        nc.scalar.copy(u_sb[:, PAD:U_S], ps[:, :])
                        nc.scalar.copy(g_in[:, i, 0:CTX], ps[:, SEQ - CTX:SEQ]).then_inc(act_u, 1)
                        segs = u_sb[:, U_S:UW].rearrange("p (b s) -> p b s", s=SEG)
                        act.wait_ge(act_b7, g * B7 + 2)
                        nc.scalar.copy(segs[:, :, 0:CTX], st_t[:, i, :].rearrange("p (b s) -> p b s", s=CTX))
                        act.wait_ge(pe_b7, b7_at)
                        nc.scalar.copy(segs[:, :, CTX:SEG], b7[:, 0:TS].rearrange("p (b s) -> p b s", s=NQ))
                        nc.scalar.copy(g_in[:, i, CTX:GC], b7[:, 0:TS]).then_inc(act_b7, 1)
                    if kind == "z" and i == 0:
                        act.wait_ge(pe_b7, g * B7 + (B7 + B7_AT["g", 0] + 1))
                        act.wait_ge(go_free, g + 1)
                        nc.scalar.copy(g_out[:, :], b7[0:GC, :]).then_inc(act_b7, 1)
                    if kind == "z":
                        act.wait_ge(tile_done, g * NCH + (n + 1 + CR_W))
                        act.wait_ge(dve_m, g * 4 + (i + 1))
                        if i == 0:
                            act.wait_ge(dve_pool, g * 4 + 5)
                        nc.scalar.activation(t2[:, 0:SEQ], ps[:, :], ACT.Silu).then_inc(act_z, 1)
                        act.wait_ge(pe_b7, b7_at)
                        nc.scalar.activation(sz_s[:, :], b7[:, 0:TS], ACT.Silu).then_inc(act_b7, 1)
                    if kind == "m":
                        act.wait_ge(pe_b7, b7_at)
                        nc.scalar.activation(ym_s[:, :], b7[:, 0:TS], ACT.Copy,
                                             scale=sc_t[:, bass.ds(g * 4 + i, 1)]).then_inc(act_b7, 1)

            norm(0)
            act.wait_ge(ld_w[0], 16)
            hi(0, 0, w_raw[0])
            with act.Fori(0, NG - 1) as g:
                group(g, False)
            group(NG - 1, True)
            norm(1)

            act.wait_ge(ld_wf, 16)
            hi(C_L0, 0, wf[:, :, :].rearrange("p k n -> p (k n)"))
            px(C_L0 + 1 + CR_W)
            act.wait_ge(ld_w[0], 16 * 33)
            hi(C_L0 + 1, 1, w_raw[0])
            act.wait_ge(tile_done, C_L0 + 1 + CR_W)
            nc.scalar.activation(lf[0][:, 0:SEQ], ps_a[0:NH, :], ACT.Identity, bias=bf_t[:, :]).then_inc(act_t, 1)
            act.wait_ge(pe_b7, B7 + B7_L0 + 1)
            nc.scalar.activation(lf[0][:, SEQ:LW], b7[0:NH, 0:TS], ACT.Identity, bias=bf_t[:, :]).then_inc(act_b7, 1)
            act.wait_ge(dve_lf, 1)
            nc.scalar.activation(lf[1][:, :], lf[1][:, :], ACT.Exp, scale=-1.0).then_inc(act_lf, 1)
            act.wait_ge(dve_lf, 2)
            nc.scalar.activation(lf[2][:, :], lf[2][:, :], ACT.Ln).then_inc(act_lf, 1)

            def proj(f, last):
                for n in range(4):
                    px(f * 4 + (C_L0 + 2 + n + CR_W))
                    if not (last and n == 3):
                        act.wait_ge(ld_w[(n + 1) % 2], f * 32 + 16 * (33 + (n + 1) // 2))
                        hi(f * 4 + (C_L0 + 2 + n), n % 2, w_raw[(n + 1) % 2])
                    ps = tile_ps((n + 1) % 2)
                    act.wait_ge(tile_done, f * 4 + (C_L0 + 2 + n + CR_W))
                    b7_at = f * 6 + (B7 + B7_L0 + 1 + (0, 1, 2, 4)[n] + 1)
                    if n < 3:
                        act.wait_ge(pool_free, f + 1)
                    if n == 0:
                        nc.scalar.mul(q_st[:, :], ps[:, :], QSCALE).then_inc(act_t, 1)
                        act.wait_ge(pe_b7, b7_at)
                        nc.scalar.mul(q_s[:, bass.ds(f, 1), :].rearrange("p o n -> p (o n)"), b7[:, 0:TS], QSCALE)\
                          .then_inc(act_b7, 1)
                    elif n == 1:
                        nc.scalar.copy(k_st[:, :], ps[:, :]).then_inc(act_t, 1)
                        act.wait_ge(pe_b7, b7_at)
                        nc.scalar.copy(ks_st[:, :], b7[:, 0:TS])
                        nc.scalar.copy(k_s[:, bass.ds(f, 1), :].rearrange("p o n -> p (o n)"), b7[:, 0:TS])\
                          .then_inc(act_b7, 1)
                    elif n == 2:
                        nc.scalar.copy(v_st[:, :], ps[:, :]).then_inc(act_t, 1)
                        act.wait_ge(pe_b7, b7_at)
                        nc.scalar.copy(vs_st[:, :], b7[:, 0:TS]).then_inc(act_b7, 1)
                        act.wait_ge(pe_b7, b7_at + 1)
                        nc.scalar.copy(ks_tm[:, bass.ds(f * P, P)], b7[0:TS, 0:P]).then_inc(act_b7, 1)
                    else:
                        act.wait_ge(spill, 16)
                        act.wait_ge(dve_xn, 18)
                        nc.scalar.activation(z_t[:, bass.ds(f, 1), 0:SEQ].rearrange("p o n -> p (o n)"), ps[:, :],
                                             ACT.Silu).then_inc(act_t, 1)
                        act.wait_ge(pe_b7, b7_at)
                        nc.scalar.activation(z_t[:, bass.ds(f, 1), SEQ:SEQ + TS].rearrange("p o n -> p (o n)"),
                                             b7[:, 0:TS], ACT.Silu).then_inc(act_b7, 1)
                        act.wait_ge(pe_b7, b7_at + 1)
                        nc.scalar.copy(vs_tm[:, bass.ds(f * P, P)], b7[0:TS, 0:P]).then_inc(act_b7, 1)

            with act.Fori(0, KT8 - 1) as f:
                proj(f, False)
            proj(KT8 - 1, True)

        @block.tensor
        def _(pe):
            pe.sem_inc(smp_used, CR_W)
            pe.sem_inc(tile_done, CR_W)
            pe.sem_inc(pe_b7, B7)
            pe.wait_ge(dve_cst, 1)

            def norm(n):
                for f in range(16):
                    k, half = f % 8, f // 8
                    pe.wait_ge(dve_xn, 9 * n + 4 * (half + 1))
                    if 16 * n + f >= 2:
                        pe.wait_ge(dve_nt, 16 * n + f - 1)
                    for i in range(4):
                        mm = nc.tensor.transpose(out_b[f % 2][:, P * i:P * i + P],
                                                 xn[:, 4 * half + i, P * k:P * k + P], ident)
                    mm.then_inc(pe_nt, 1)
                pe.wait_ge(dve_xn, 9 * n + 9)
                if n:
                    pe.wait_ge(dve_px, 1 + NG * 4)
                for k in range(KT8):
                    mm = nc.tensor.transpose(b6[:, TS * k:TS * k + TS], xn_s[:, P * k:P * k + P], con[0:TS, C_ID:C_ID + TS])
                mm.then_inc(pe_nts, 1)
                pe.wait_ge(dve_nt, 16 * n + 16)
                pe.wait_ge(dve_nts, n + 1)

            def three(ps, pairs):
                last = len(pairs) - 1
                for j, (ah, al, bh, bl) in enumerate(pairs):
                    nc.tensor.matmul(ps, ah, bh, start=j == 0, stop=False)
                    nc.tensor.matmul(ps, ah, bl, start=False, stop=False)
                    mm = nc.tensor.matmul(ps, al, bh, start=False, stop=j == last)
                return mm

            def sample_tile(raw, acts, nk):
                for k in range(nk):
                    q = k % 4
                    mm = nc.tensor.matmul(b6[32 * q:32 * q + TS, 0:P], acts[:, k, :], raw[:, P * k:P * k + P],
                                          start=k < 4, stop=k >= nk - 4, tile_position=(0, 32 * q))
                mm.then_inc(smp_used, 1)

            def prompt_tile(ps, slot, hi, lo, nk):
                for half in range(2):
                    c = slice(512 * half, 512 * half + 512)
                    mm = three(ps[:, c], [(w_hi[slot][:, P * k:P * k + P], w_lo[slot][:, P * k:P * k + P],
                                           hi[:, k, c], lo[:, k, c]) for k in range(nk)])
                mm.then_inc(tile_done, 1)

            def add_parts():
                nc.tensor.matmul(b7[:, 0:TS], px_sb[:, :], sum4, start=True, stop=True).then_inc(pe_b7, 1)

            norm(0)
            with pe.Fori(0, NG) as g:
                pe.wait_ge(ld_st, g * 16 + 16)
                pe.wait_ge(act_b7, g * B7 + 1)
                for i in range(4):
                    mm = nc.tensor.transpose(b7[:, 120 * i:120 * i + 120], st_in[:, P * i:P * i + P],
                                             con[0:120, C_ID:C_ID + 120])
                mm.then_inc(pe_b7, 1)
                for n, (kind, i) in enumerate(CHUNKS):
                    slot, raw = n % 2, w_raw[n % 2]
                    t = before("uzm", n)
                    pe.wait_ge(ld_w[slot], g * 128 + 16 * (n // 2 + 1))
                    pe.wait_ge(act_px, g * 12 + (t + 1))
                    pe.wait_ge(dve_px, g * 4 + (before("o", n) + 1))
                    if kind == "m":
                        pe.wait_ge(dve_pool, g * 4 + 5)
                        sample_tile(raw, p_s, 4)
                    elif kind == "o":
                        pe.wait_ge(dve_m, g * 4 + (2 * (i // 2 + 1) + 1))
                        for k in range(2):
                            mm = nc.tensor.matmul(b6[32 * k:32 * k + TS, :], y_s[:, k, :], raw[:, 512 * k:512 * k + 512],
                                                  start=True, stop=True, tile_position=(0, 32 * k))
                        mm.then_inc(smp_used, 1)
                    else:
                        sample_tile(raw, h_s, KT8)
                    pe.wait_ge(dve_lo, g * NCH + (n + 1 + CR_W))
                    if kind == "o":
                        for u in range(TT):
                            pe.wait_ge(dve_o, g * 32 + (8 * i + u + 1))
                            r = slice(P * u, P * u + P)
                            mm = three(out_b[u % 2][:, :], [(y_hi[:, k, r], y_lo[:, k, r],
                                                             w_hi[slot][:, 512 * k:512 * k + 512],
                                                             w_lo[slot][:, 512 * k:512 * k + 512]) for k in range(2)])
                            mm.then_inc(pe_o if u < TT - 1 else tile_done, 1)
                        continue
                    free = {0: (act_z, 1), 1: (dve_mf, 1), 2: (act_u, 1), 3: (act_u, 2), 4: (act_u, 3),
                            5: (act_u, 4), 6: (act_z, 2), 7: (dve_mf, 2), 8: (act_z, 3), 9: (dve_mf, 3),
                            10: (act_z, 4), 11: (dve_mf, 4)}[t]
                    pe.wait_ge(free[0], g * 4 + free[1])
                    if (kind, i) == ("z", 0):
                        pe.wait_ge(act_b7, g * B7 + (1 + B7_AT["g", 0]))
                    if kind == "m":
                        prompt_tile(tile_ps(t % 2), slot, po_hi, po_lo, 4)
                    else:
                        prompt_tile(tile_ps(t % 2), slot, h_hi, h_lo, KT8)
                    if (kind, i) == ("z", 0):
                        for j in range(4):
                            mm = nc.tensor.transpose(b7[0:GC, P * j:P * j + P], g_in[:, j, :], ident)
                        mm.then_inc(pe_b7, 1)
                    pe.wait_ge(act_px, g * 12 + (t + 2))
                    pe.wait_ge(act_b7, g * B7 + (1 + B7_AT[kind, i]))
                    add_parts()
            norm(1)

            pe.wait_ge(ld_wf, 16)
            sample_tile(wf[:, :, :].rearrange("p k n -> p (k n)"), h_s, KT8)
            pe.wait_ge(dve_lo, C_L0 + 1 + CR_W)
            prompt_tile(ps_a, 0, h_hi, h_lo, KT8)
            pe.wait_ge(act_px, 1 + PX_L0 + 1)
            add_parts()
            with pe.Fori(0, KT8) as f:
                for n in range(4):
                    b7_at = f * 6 + (1 + B7_L0 + 1 + (0, 1, 2, 4)[n])
                    pe.wait_ge(ld_w[n % 2], f * 32 + 16 * (33 + n // 2))
                    pe.wait_ge(act_px, f * 4 + (1 + PX_L0 + 1 + n))
                    sample_tile(w_raw[n % 2], h_s, KT8)
                    pe.wait_ge(dve_lo, f * 4 + (C_L0 + 2 + n + CR_W))
                    pe.wait_ge(act_t, f * 4 + (n + 1))
                    prompt_tile(tile_ps((n + 1) % 2), (n + 1) % 2, h_hi, h_lo, KT8)
                    pe.wait_ge(act_px, f * 4 + (1 + PX_L0 + 2 + n))
                    pe.wait_ge(act_b7, b7_at)
                    add_parts()
                    if n < 2:
                        continue
                    src, src_s = (k_st, ks_st) if n == 2 else (v_st, vs_st)
                    pe.wait_ge(act_t, f * 4 + (n + 2))
                    for j in range(2):
                        pe.wait_ge(dve_tm, f * 4 + (2 * (n - 2) + j + 1))
                        for i in range(4):
                            r = P * (4 * j + i)
                            mm = nc.tensor.transpose(out_b[j][:, P * i:P * i + P], src[:, r:r + P], ident)
                        mm.then_inc(pe_tm, 1)
                    pe.wait_ge(act_b7, b7_at + 1)
                    nc.tensor.transpose(b7[0:TS, 0:P], src_s[:, :], ident).then_inc(pe_b7, 1)

            pe.wait_ge(dve_tot, 2)
            for t in range(2):
                mm = nc.tensor.matmul(b6[:, NH * t:NH * t + NH], con[:, C_TRI:C_TRI + P], tot[:, t, :], start=True, stop=True)
            mm.then_inc(pe_tail, 1)
            pe.wait_ge(dve_lf, 7)
            pe.wait_ge(dve_tm, 2 + 4 * KT8)
            for i in range(TT):
                nc.tensor.transpose(b4[:, NH * i:NH * i + NH], lf[0][:, P * i:P * i + P], con[0:NH, C_ID:C_ID + NH])
            nc.tensor.transpose(b4[0:TS, 256:256 + NH], lf[0][:, SEQ:LW], con[0:NH, C_ID:C_ID + NH])
            nc.tensor.matmul(b5[:, 0:TS], con[0:NH, C_SEL:C_SEL + P], c_s[:, :], start=True, stop=True).then_inc(pe_tail, 1)

        @block.vector
        def _(dve):
            chain = [0]

            def link(ins):
                chain[0] += 1
                ins.then_inc(dve_c, 1)
                dve.wait_ge(dve_c, chain[0])

            V = nc.vector
            for s_, n_ in ((dve_lo, CR_W), (dve_px, 1), (dve_pool, 1), (dve_m, 1), (dve_mf, 1), (dve_o, 2), (dve_tm, 2)):
                dve.sem_inc(s_, n_)
            dve.wait_ge(ld_small, N_SMALL)
            V.memset(ss[:, :], 1.0)
            V.memset(ones[:, :], 1.0)
            V.memset(u_sb[:, 0:PAD], 0.0)
            V.memset(q_bd[:, :, :], 0.0)
            V.tensor_copy(ident_b[:, :], ident)
            V.memset(x_s[32:64, :], 0.0)
            V.tensor_copy(caus_b[:, :], con[:, C_CAUS:C_CAUS + P]).then_inc(dve_cst, 1)
            dve.wait_ge(dve_cst, 1)

            def norm(n):
                dve.wait_ge(ld_x, 48)
                link(V.tensor_copy(xn_s[:, :], x_s[32:64, :]))
                V.tensor_tensor(xt_s[:, :], x_s[0:TS, :], xn_s[:, :], ALU.add).then_inc(dve_xt, 1)
                dve.wait_ge(act_ss, n + 1)
                V.tensor_scalar(ss[:, :], ss[:, :], 1.0 / DM, EPS, ALU.mult, ALU.add).then_inc(dve_var, 1)
                dve.wait_ge(act_sq, n + 1)
                link(V.reciprocal(ss[:, :], ss[:, :]))
                for i in range(TT):
                    V.tensor_scalar(xn[:, i, :], x_p[:, i, :], ss[:, i:i + 1], None, ALU.mult).then_inc(dve_xn, 1)
                V.tensor_scalar(xn_s[:, :], xt_s[:, :], ss[0:TS, TT:TT + 1], None, ALU.mult).then_inc(dve_xn, 1)
                for f in range(16):
                    k, half = f % 8, f // 8
                    dve.wait_ge(act_nt, 16 * n + f + 1)
                    c = slice(512 * half, 512 * half + 512)
                    V.scalar_tensor_tensor(h_lo[:, k, c], out_b[f % 2][:, :], g_t[:, n, k:k + 1],
                                           h_hi[:, k, c].bitcast(F32), ALU.mult, ALU.subtract).then_inc(dve_nt, 1)
                dve.wait_ge(pe_nts, n + 1)
                for k in range(KT8):
                    last = V.tensor_scalar(h_s[:, k, :], b6[:, TS * k:TS * k + TS], g_t[:, n, k:k + 1], None, ALU.mult)
                last.then_inc(dve_nts, 1)

            def lo(c, slot, raw, width=1024):
                dve.wait_ge(act_hi, c + 1)
                V.tensor_tensor(w_lo[slot][:, 0:width], raw[:, 0:width], w_hi[slot][:, 0:width].bitcast(F32),
                                ALU.subtract).then_inc(dve_lo, 1)

            def pool_tile(g, i):
                w = WINDOWS[g]
                dve.wait_ge(act_u, 4 * g + i + 1)
                dve.wait_ge(act_b7, 1 + B7 * g + 2 + i)
                cur, nxt, d, first = u_sb, t1, 1, 1
                while d < w:
                    link(V.tensor_tensor(nxt[:, first:UW], cur[:, first:UW], cur[:, first - d:UW - d], ALU.add))
                    cur, nxt = nxt, (t2 if nxt is t1 else t1)
                    d *= 2
                    first += d
                link(V.scalar_tensor_tensor(nxt[:, PAD:UW], cur[:, PAD:UW], 1.0 / w, u_sb[:, PAD:UW], ALU.mult, ALU.subtract))
                e = slice(PAD, PAD + w - 1)
                link(V.tensor_tensor(nxt[:, e], cur[:, e], con[:, C_INV:C_INV + w - 1], ALU.mult))
                link(V.tensor_tensor(nxt[:, e], nxt[:, e], u_sb[:, e], ALU.subtract))
                link(V.tensor_copy(po_hi[:, i, :], nxt[:, PAD:U_S]))
                V.tensor_copy(p_s[:, i, :].rearrange("p (b q) -> p b q", q=NQ),
                              nxt[:, U_S:UW].rearrange("p (b s) -> p b s", s=SEG)[:, :, CTX:SEG])
                link(V.tensor_tensor(po_lo[:, i, :], nxt[:, PAD:U_S], po_hi[:, i, :].bitcast(F32), ALU.subtract))
                dve.sem_inc(dve_pool, 1)

            def mix_tile(g, n, d):
                dve.wait_ge(tile_done, NCH * g + n + 1 + CR_W)
                dve.wait_ge(act_z, 4 * g + d + 2)
                ps = tile_ps(before("uzm", n) % 2)
                V.scalar_tensor_tensor(t1[:, 0:SEQ], ps[:, :], sc_t[:, 4 * g + d:4 * g + d + 1], t2[:, 0:SEQ],
                                       ALU.mult, ALU.mult).then_inc(dve_mf, 1)
                dve.wait_ge(dve_mf, 4 * g + d + 2)
                link(V.tensor_copy(y_hi[:, d % 2, :], t1[:, 0:SEQ]))
                link(V.tensor_tensor(y_lo[:, d % 2, :], t1[:, 0:SEQ], y_hi[:, d % 2, :].bitcast(F32), ALU.subtract))
                dve.wait_ge(act_b7, 1 + B7 * g + B7_AT["m", d] + 1)
                V.tensor_tensor(y_s[:, d % 2, :], ym_s[:, :], sz_s[:, :], ALU.mult).then_inc(dve_m, 1)

            def out_piece(g, n, j):
                c = NCH * g + n
                half = slice(512 * (j % 2), 512 * (j % 2) + 512)
                dve.wait_ge(smp_used, c + 1 + CR_W)
                V.tensor_tensor(x_s[:, half], x_s[:, half], b6[0:64, :], ALU.add).then_inc(dve_px, 1)
                for u in range(TT):
                    if u < TT - 1:
                        dve.wait_ge(pe_o, (4 * g + j) * (TT - 1) + u + 1)
                    else:
                        dve.wait_ge(tile_done, c + 1 + CR_W)
                    V.tensor_tensor(x_p[:, u, half], x_p[:, u, half], out_b[u % 2][:, :], ALU.add).then_inc(dve_o, 1)

            norm(0)
            lo(0, 0, w_raw[0])
            for g in range(NG):
                for n, (kind, i) in enumerate(CHUNKS):
                    if n < NCH - 1 or g < NG - 1:
                        nxt = CHUNKS[(n + 1) % NCH][0]
                        lo(NCH * g + n + 1, (n + 1) % 2, w_raw[(n + 1) % 2], 512 if nxt == "m" else 1024)
                    if kind == "u":
                        pool_tile(g, i)
                    elif kind == "m":
                        mix_tile(g, n, i)
                    elif kind == "o":
                        out_piece(g, n, i)
            V.memset(wf[:, :, :], 0.0).then_inc(dve_wf, 1)
            norm(1)
            dve.wait_ge(ld_wf, 16)
            lo(C_L0, 0, wf[:, :, :].rearrange("p k n -> p (k n)"))
            lo(C_L0 + 1, 1, w_raw[0])

            A, B, C, D, M = lf

            def log_forget_start():
                dve.wait_ge(act_t, 2)
                dve.wait_ge(act_b7, 1 + B7_L0 + 1)
                V.scalar_tensor_tensor(B[:, :], A[:, :], -1.0, A[:, :], ALU.mult, ALU.max).then_inc(dve_lf, 1)
                dve.wait_ge(act_lf, 1)
                link(V.tensor_scalar(C[:, :], B[:, :], 1.0, None, ALU.add))
                link(V.tensor_scalar(D[:, :], C[:, :], -1.0, None, ALU.add))
                link(V.tensor_scalar(M[:, :], D[:, :], 0.0, None, ALU.is_equal))
                V.tensor_tensor(D[:, :], D[:, :], M[:, :], ALU.add).then_inc(dve_lf, 1)

            def log_forget():
                dve.wait_ge(dve_lf, 2)
                link(V.reciprocal(D[:, :], D[:, :]))
                dve.wait_ge(act_lf, 2)
                link(V.tensor_tensor(C[:, :], C[:, :], M[:, :], ALU.add))
                link(V.tensor_tensor(C[:, :], C[:, :], D[:, :], ALU.mult))
                link(V.tensor_tensor(B[:, :], B[:, :], C[:, :], ALU.mult))
                V.scalar_tensor_tensor(A[:, :], A[:, :], 0.0, B[:, :], ALU.min, ALU.subtract).then_inc(dve_lf, 1)
                V.memset(D[:, 0:SEQ], 1.0).then_inc(dve_lf, 1)
                dve.wait_ge(dve_lf, 4)
                V.tensor_tensor_scan(B[:, 0:SEQ], D[:, 0:SEQ], A[:, 0:SEQ], 0.0, ALU.mult, ALU.add).then_inc(dve_lf, 1)
                dve.wait_ge(dve_lf, 5)
                V.tensor_scalar(C[:, 0:SEQ], B[:, 0:SEQ], -1.0, None, ALU.mult).then_inc(dve_lf, 1)
                new = A[:, SEQ:LW].rearrange("p (b q) -> p b q", q=NQ)
                run = c_s[:, :].rearrange("p (b q) -> p b q", q=NQ)
                link(V.tensor_copy(c_s[:, :], A[:, SEQ:LW]))
                for q in range(1, NQ):
                    link(V.tensor_tensor(run[:, :, q], run[:, :, q - 1], new[:, :, q], ALU.add))
                dve.sem_inc(dve_lf, 1)

            def page_sums(t):
                dve.wait_ge(ld_lp[t], 16)
                by_head = lp[:, :].rearrange("p (k h) -> p k h", h=NH)
                for h in range(NH):
                    last = V.tensor_tensor_scan(pfx[t][:, h, :], ones[:, :], by_head[:, :, h], 0.0, ALU.mult, ALU.add)
                link(last)
                V.tensor_copy(tot[:, t, :], pfx[t][:, :, PAGE - 1]).then_inc(dve_tot, 1)

            log_forget_start()
            for f in range(KT8):
                for n in range(4):
                    if f < KT8 - 1 or n < 3:
                        lo(C_L0 + 2 + 4 * f + n, n % 2, w_raw[(n + 1) % 2])
                    if f == 0 and n == 0:
                        log_forget()
                    if n >= 2:
                        dve.wait_ge(pool_free, f + 1)
                        for j in range(2):
                            dve.wait_ge(pe_tm, 4 * f + 2 * (n - 2) + j + 1)
                            V.tensor_copy((k_tm, v_tm)[n - 2][:, 4 * j:4 * j + 4, :].rearrange("p t n -> p (t n)"),
                                          out_b[j][:, :]).then_inc(dve_tm, 1)
                if f in (3, 5):
                    page_sums((f - 3) // 2)

            dve.wait_ge(pe_tail, 1)
            link(V.tensor_tensor(tot[:, :, :].rearrange("p t h -> p (t h)"), tot[:, :, :].rearrange("p t h -> p (t h)"),
                                 b6[:, 0:2 * NH], ALU.add))
            for t in range(2):
                for h in range(NH):
                    last = V.tensor_scalar(pfx[t][:, h, :], pfx[t][:, h, :], -1.0, tot[:, t, h:h + 1], ALU.mult, ALU.add)
                last.then_inc(dve_dec, 1)
            dve.wait_ge(pe_tail, 2)
            V.tensor_copy(lf_tm[:, :, :].rearrange("p t h -> p (t h)"), b4[:, 0:TT * NH])
            V.tensor_copy(lfs_tm[:, :], b4[0:TS, 256:256 + NH]).then_inc(dve_tail, 1)
            link(V.tensor_copy(cr_sb[:, :], b5[:, 0:TS]))
            cr_b = cr_sb[:, :].unsqueeze(1).to_broadcast([P, NB, TS])
            link(V.tensor_tensor(mq_w[:, :, :], con[:, C_MQ:C_MQ + NB * TS].rearrange("p (b t) -> p b t", t=TS), cr_b, ALU.mult))
            V.tensor_reduce(cq[:, :], mq_w[:, :, :], AX, ALU.add)
            V.tensor_tensor(d_new[:, :, :], con[:, C_NEG:C_NEG + NB * TS].rearrange("p (b t) -> p b t", t=TS), cr_b,
                            ALU.subtract).then_inc(dve_tail, 1)

        dense.__exit__(None, None, None)

        SLOTS = 8
        HALF = 2 * PAGE
        pt_n = place("pt_n", [TS, P], F32, at_px)
        sm_p = place("sm_p", [P, DM], F32, big_at(19456))
        xs_c = place("xs_c", [TS, DM], F32, big_at(24608))

        def t2_uses(prompt, sample):
            uses = []
            for s in range(SLOTS):
                if sample:
                    uses.append(("s", s))
                    if s == SLOTS - 1:
                        uses.append(("n", s))
                if prompt:
                    for h in range(2):
                        uses += [(h, s, f) for f in range((QBLOCKS[s] + 4) // 4)]
            return uses

        T2_FIRST, T2_BOTH, T2_LAST = t2_uses(True, False), t2_uses(True, True), t2_uses(False, True)

        def t2_at(b, key):
            if isinstance(b, int) and b == 0:
                return T2_FIRST.index(key)
            if isinstance(b, int) and b == NB:
                return len(T2_FIRST) + (NB - 1) * len(T2_BOTH) + T2_LAST.index(key)
            return b * len(T2_BOTH) + (len(T2_FIRST) - len(T2_BOTH) + T2_BOTH.index(key))

        def past(eng, semaphore, n):
            if not isinstance(n, int) or n > 0:
                eng.wait_ge(semaphore, n)

        k_full = [sem(f"k_full{r}") for r in range(KR)]
        v_full = [sem(f"v_full{r}") for r in range(VR)]
        ld_qk, ld_v, ld_os, ld_fn, st_o, st_y, o_free = (
            sem(n) for n in ("ld_qk", "ld_v", "ld_os", "ld_fn", "st_o", "st_y", "o_free"))
        ld_d = [sem("ld_d0"), sem("ld_d1")]
        ld_x1 = [sem(f"ld_x1_{i}") for i in range(3)]
        pe_s, pe_kt, pe_t2, pe_qk, pe_new = (sem(n) for n in ("pe_s", "pe_kt", "pe_t2", "pe_qk", "pe_new"))
        pe_pvp, pe_pv, pe_vo, pe_y, pe_sm = (sem(n) for n in ("pe_pvp", "pe_pv", "pe_vo", "pe_y", "pe_sm"))
        act_kt, act_p, act_t2, act_e, act_y, act_r = (
            sem(n) for n in ("act_kt", "act_p", "act_t2", "act_e", "act_y", "act_r"))
        dve_kt, dve_mx, dve_pn, dve_s, dve_op = (sem(n) for n in ("dve_kt", "dve_mx", "dve_pn", "dve_s", "dve_op"))
        dve_q, dve_nm, dve_ov, dve_d0, dve_y = (sem(n) for n in ("dve_q", "dve_nm", "dve_ov", "dve_d0", "dve_y"))
        dve_v, dve_n, dve_sm, dve_ca, dve_cv, dve_ce = (
            sem(n) for n in ("dve_v", "dve_n", "dve_sm", "dve_ca", "dve_cv", "dve_ce"))

        with nc.Block() as attend:

            @attend.sync
            def _(sp):
                def k_page(b, p):
                    page = sp.value_load(pt_sb[0:1, bass.ds(b * PAGES + p, 1)], min_val=0, max_val=n_phys - 1)
                    past(sp, pe_kt, b * 64 + 4 * (p // 2 - 3))
                    sp.dma_start(k_pg[:, p % KR, :], cache_k[0, bass.ds(page, 1)].rearrange("o k h d -> (o k) (h d)"))\
                      .then_inc(k_full[p % KR], 16)

                def v_page(b, p):
                    page = sp.value_load(pt_sb[0:1, bass.ds(b * PAGES + (p - PAGES), 1)], min_val=0, max_val=n_phys - 1)
                    sp.wait_ge(pe_pv, b * PAGES + (p - PAGES + 1))
                    sp.dma_start(v_pg[:, p % VR, :], cache_v[0, bass.ds(page, 1)].rearrange("o k h d -> (o k) (h d)"))\
                      .then_inc(v_full[p % VR], 16)

                for p in range(PAGES):
                    k_page(0, p)
                with sp.Fori(1, NB) as b:
                    for p in range(PAGES):
                        k_page(b, p)
                        v_page(b, p)
                for p in range(PAGES):
                    v_page(NB, p)
                    if p < KT8:
                        if p == 0:
                            sp.wait_ge(pe_kt, NB * 64)
                        sp.dma_start(w_o[:, p, :], w_out_attn[0, P * p:P * p + P, :]).then_inc(k_full[p], 16)
                sp.wait_ge(st_y, 16 * (TT + 1))

            @attend.gpsimd
            def _(pool):
                def decay_half(b, half):
                    c = slice(half * (PAST // 2), (half + 1) * (PAST // 2))
                    for j in range(4):
                        src = decay[bass.ds(b, 1), 4 * j:4 * j + 4, c].rearrange("o h c -> (o h) c")
                        pool.dma_start(d_sb[32 * j:32 * j + 16, c],
                                       src.unsqueeze(1).to_broadcast([4, NQ, PAST // 2])).then_inc(ld_d[half], 16)

                def qk_pair(b):
                    for src, dst in ((q_aug, qa), (k_aug, ka)):
                        pool.dma_start(dst[:, :, :], src[bass.ds(b * 2, 2), :, :].rearrange("h d t -> d h t"))\
                            .then_inc(ld_qk, 16)

                def v_pair(b):
                    pool.dma_start(v_pr[:, :, :], v_prompt[0, 0].rearrange("(t p) h d -> p t (h d)", p=P)
                                   [:, :, bass.ds(b * P, P)]).then_inc(ld_v, 16)

                def following(b):
                    pool.wait_ge(dve_s, b * 9 + 4)
                    hold(pool)
                    decay_half(b + 1, 0)
                    pool.wait_ge(pe_s, b * 16 + 16)
                    hold(pool)
                    qk_pair(b + 1)
                    pool.wait_ge(pe_pvp, b * 16 + 16)
                    hold(pool)
                    v_pair(b + 1)
                    pool.wait_ge(dve_s, b * 9 + 8)
                    hold(pool)
                    decay_half(b + 1, 1)

                def sample_out(b):
                    pool.wait_ge(dve_ov, b + 1)
                    hold(pool)
                    for j in range(4):
                        pool.dma_start(o_smp[bass.ds(b * NQ - NQ, NQ), 256 * j:256 * j + 256]
                                       .rearrange("q (h d) -> h q d", d=HD),
                                       o_n[32 * j:32 * j + 16, :]).then_inc(st_o, 16)
                    pool.wait_ge(st_o, b * 64)
                    pool.sem_inc(o_free, 1)

                pool.sem_inc(o_free, 1)
                qk_pair(0)
                v_pair(0)
                pool.wait_ge(dve_d0, 1)
                decay_half(0, 0)
                decay_half(0, 1)
                following(0)
                with pool.Fori(1, NB - 1) as b:
                    following(b)
                    sample_out(b)
                pool.wait_ge(pe_s, NB * 16)
                pool.dma_start(fn_b[:, :], final_norm.unsqueeze(0).to_broadcast([P, DM])).then_inc(ld_fn, 16)
                pool.wait_ge(pe_new, NB)
                for i in range(3):
                    pool.dma_start(x1_t[i][:, :], x1_scr[P * i:P * i + P, :]).then_inc(ld_x1[i], 16)
                sample_out(NB - 1)
                for i in range(TT):
                    if i == 5:
                        sample_out(NB)
                        pool.wait_ge(st_o, 64 * NB)
                        pool.dma_start(os_tm[:, :], o_smp[:, :]).then_inc(ld_os, 16)
                    pool.wait_ge(dve_n, i + 1)
                    pool.dma_start(y_prompt[0, P * i:P * i + P, :], x1_t[i % 3][:, :]).then_inc(st_y, 16)
                    if i + 3 < TT:
                        pool.wait_ge(st_y, 16 * (i + 1))
                        r = P * (i + 3)
                        pool.dma_start(x1_t[i % 3][:, :], x1_scr[r:r + P, :]).then_inc(ld_x1[i % 3], 16)
                pool.wait_ge(dve_n, TT + 1)
                pool.dma_start(y_sample.rearrange("b q d -> (b q) d"), xs_c[:, :]).then_inc(st_y, 16)

            @attend.tensor
            def _(pe):
                def scores(b, s, h):
                    qb = QBLOCKS[s]
                    if s == 0 and h == 0:
                        pe.wait_ge(ld_qk, b * 32 + 32)
                    past(pe, act_p, b * 16 + (2 * s + h))
                    for c in range(0, qb + 1, 4):
                        end = min(c + 4, qb + 1)
                        nc.tensor.matmul(ps_a[:, P * c:P * end], qa[:, h, P * qb:P * qb + P], ka[:, h, P * c:P * end],
                                         start=True, stop=end <= qb)
                    nc.tensor.matmul(ps_a[:, P * qb:P * qb + P], ident_b[:, :], caus_b[:, :], start=False, stop=True)\
                        .then_inc(pe_s, 1)

                def k_turn(b, s, h):
                    p = 4 * s + 2 * h
                    for i in range(2):
                        pe.wait_ge(k_full[(p + i) % KR], b * 64 + 16 * ((p + i) // KR + 1))
                    for m in range(4):
                        bank, free = ((b4, act_kt), (b5, dve_kt))[m % 2]
                        if s == 0 and h == 0 and m == 1:
                            past(pe, dve_s, b * 9)
                        past(pe, free, b * 32 + (4 * s + 2 * h + m // 2))
                        for j in range(2):
                            for i in range(2):
                                c = HALF * j + PAGE * i
                                f = P * (2 * m + j)
                                mm = nc.tensor.transpose(bank[:, c:c + PAGE], k_pg[:, (p + i) % KR, f:f + P], ident)
                        mm.then_inc(pe_kt, 1)

                def sample_scores(b, s, h):
                    if h == 0:
                        past(pe, dve_s, b * 9 + s)
                    if h == 0 and s == 0:
                        pe.wait_ge(dve_q, b + 1)
                    pe.wait_ge(act_kt, b * 32 + (4 * s + 2 * h + 2))
                    pe.wait_ge(dve_kt, b * 32 + (4 * s + 2 * h + 2))
                    for pr in range(KT8):
                        r = 32 * (pr // 2)
                        mm = nc.tensor.matmul(b7[r:r + 32, HALF * h:HALF * h + HALF], q_bd[:, pr, :], kt[h][:, pr, :],
                                              start=pr % 2 == 0, stop=pr % 2 == 1, tile_position=(0, r))
                    mm.then_inc(pe_qk, 1)

                def new_scores(b):
                    pe.wait_ge(dve_kt, b * 32 + 32)
                    for pr in range(KT8):
                        r = 32 * (pr // 2)
                        mm = nc.tensor.matmul(b5[r:r + 32, 0:TS], q_bd[:, pr, :], k_s[:, pr, :],
                                              start=pr % 2 == 0, stop=pr % 2 == 1, tile_position=(0, r))
                    mm.then_inc(pe_new, 1)

                def prompt_turn(b, s, h):
                    pe.wait_ge(dve_pn, b * 16 + (2 * s + h + 1))
                    for f in range((QBLOCKS[s] + 4) // 4):
                        past(pe, act_t2, t2_at(b, (h, s, f)))
                        for i in range(min(4, QBLOCKS[s] + 1 - 4 * f)):
                            c = P * (4 * f + i)
                            mm = nc.tensor.transpose(b6[:, P * i:P * i + P], p_p[:, h, c:c + P], ident)
                        mm.then_inc(pe_t2, 1)

                def prompt_values(b, s, h):
                    if s == 0 and h == 0:
                        pe.wait_ge(ld_v, b * 16 + 16)
                    if h == 0:
                        past(pe, dve_op, b * SLOTS + s)
                    qb = QBLOCKS[s]
                    pe.wait_ge(act_t2, t2_at(b, (h, s, qb // 4)) + 1)
                    r = HD * h
                    for k in range(qb + 1):
                        mm = nc.tensor.matmul(ps_b[r:r + HD, 512:512 + P], v_pr[:, k, r:r + HD], pt_p[:, k, :],
                                              start=k == 0, stop=k == qb, tile_position=(0, r))
                    mm.then_inc(pe_pvp, 1)

                def sample_turn(b, s):
                    pe.wait_ge(act_e, b * 9 + (s + 1 - 9))
                    past(pe, act_t2, t2_at(b, ("s", s)))
                    for i in range(4):
                        c = PAGE * (4 * s + i)
                        mm = nc.tensor.transpose(b6[:, P * i:P * i + P], s_sb[:, c:c + PAGE], ident)
                    mm.then_inc(pe_t2, 1)
                    if s == SLOTS - 1:
                        pe.wait_ge(act_e, b * 9)
                        pe.wait_ge(act_t2, t2_at(b, ("n", s)))
                        nc.tensor.transpose(b6[0:TS, 0:P], s_sb[:, PAST:PAST + TS], ident).then_inc(pe_t2, 1)

                def sample_values(b, s):
                    pe.wait_ge(act_t2, t2_at(b, ("n" if s == SLOTS - 1 else "s", s)) + 1)
                    if s == 0:
                        pe.wait_ge(dve_ov, b)
                    for i in range(4):
                        p = 4 * s + i
                        pe.wait_ge(v_full[p % VR], b * 64 + (16 * (p // VR + 1) - 64))
                        for j in range(4):
                            mm = nc.tensor.matmul(ps_b[32 * j:32 * j + 32, 0:256], pt_s[:, i, 32 * j:32 * j + 32],
                                                  v_pg[:, p % VR, 256 * j:256 * j + 256],
                                                  start=p == 0, stop=False, tile_position=(0, 32 * j))
                        mm.then_inc(pe_pv, 1)
                    if s == SLOTS - 1:
                        for j in range(4):
                            mm = nc.tensor.matmul(ps_b[32 * j:32 * j + 32, 0:256], pt_n[:, 32 * j:32 * j + 32],
                                                  vs_tm[:, 256 * j:256 * j + 256],
                                                  start=False, stop=True, tile_position=(0, 32 * j))
                        mm.then_inc(pe_vo, 1)

                def batch(b, sample):
                    for s in range(SLOTS):
                        scores(b, s, 0)
                        k_turn(b, s, 0)
                        if sample:
                            sample_turn(b, s)
                        scores(b, s, 1)
                        k_turn(b, s, 1)
                        sample_scores(b, s, 0)
                        prompt_turn(b, s, 0)
                        if sample:
                            sample_values(b, s)
                        prompt_values(b, s, 0)
                        prompt_turn(b, s, 1)
                        sample_scores(b, s, 1)
                        if s == SLOTS - 1:
                            new_scores(b)
                        prompt_values(b, s, 1)

                pe.sem_inc(pe_pv, VR)
                batch(0, False)
                with pe.Fori(1, NB) as b:
                    batch(b, True)
                for i in range(TT):
                    if i < 4:
                        for s in (2 * i, 2 * i + 1):
                            sample_turn(NB, s)
                            sample_values(NB, s)
                    if i == 0:
                        pe.wait_ge(dve_op, NB * SLOTS)
                    else:
                        pe.wait_ge(dve_y, i)
                    for k in range(KT8):
                        if i == 0:
                            pe.wait_ge(k_full[k], 64 * NB + 16)
                        for half in range(2):
                            c = slice(512 * half, 512 * half + 512)
                            mm = nc.tensor.matmul(ps_a[:, c], z_t[:, k, P * i:P * i + P], w_o[:, k, c],
                                                  start=k == 0, stop=k == KT8 - 1)
                    mm.then_inc(pe_y, 1)
                    if i == 5:
                        pe.wait_ge(ld_os, 16)
                        for k in range(KT8):
                            mm = nc.tensor.transpose(b4[:, TS * k:TS * k + TS], os_tm[:, P * k:P * k + P],
                                                     con[0:TS, C_ID:C_ID + TS])
                        mm.then_inc(pe_sm, 1)
                    if i == 6:
                        pe.wait_ge(dve_sm, 1)
                        pe.wait_ge(dve_ov, NB + 1)
                        for half in range(2):
                            c = slice(512 * half, 512 * half + 512)
                            for k in range(KT8):
                                r = 32 * (k % 4)
                                mm = nc.tensor.matmul(ps_b[r:r + TS, c], h_s[:, k, :], w_o[:, k, c],
                                                      start=k < 4, stop=k >= 4, tile_position=(0, r))
                        mm.then_inc(pe_sm, 1)
                pe.wait_ge(dve_sm, 2)
                for half in range(2):
                    c = slice(512 * half, 512 * half + 512)
                    mm = nc.tensor.matmul(ps_b[0:TS, c], sum4, sm_p[:, c], start=True, stop=True)
                mm.then_inc(pe_sm, 1)

            @attend.scalar
            def _(act):
                def k_evac(b, s, h, m):
                    act.wait_ge(pe_kt, b * 64 + (8 * s + 4 * h + m + 1))
                    past(act, pe_qk, b * 16 + (2 * s + h - 1))
                    nc.scalar.copy(kt[h][:, 2 * m:2 * m + 2, :].rearrange("p a k -> p (a k)"), b4[:, :]).then_inc(act_kt, 1)

                def prompt_exp(b, s, h):
                    act.wait_ge(dve_mx, b * 16 + (2 * s + h + 1))
                    n = P * (QBLOCKS[s] + 1)
                    nc.scalar.activation(p_p[:, h, 0:n], ps_a[:, 0:n], ACT.Exp, bias=pp_nm[:, h:h + 1],
                                         accum_out=pp_l[:, h:h + 1]).then_inc(act_p, 1)

                def prompt_evac(b, s, h):
                    for f in range((QBLOCKS[s] + 4) // 4):
                        n = min(4, QBLOCKS[s] + 1 - 4 * f)
                        act.wait_ge(pe_t2, t2_at(b, (h, s, f)) + 1)
                        past(act, pe_pvp, b * 16 + (2 * s + h))
                        nc.scalar.copy(pt_p[:, 4 * f:4 * f + n, :].rearrange("p t q -> p (t q)"), b6[:, 0:P * n])\
                            .then_inc(act_t2, 1)

                def sample_exp(b, s):
                    act.wait_ge(dve_nm, b)
                    c = slice(512 * s, 512 * s + 512)
                    nc.scalar.activation(s_sb[:, c], s_sb[:, c], ACT.Exp, bias=st_nm[:, :],
                                         accum_out=st_sum[:, s:s + 1]).then_inc(act_e, 1)
                    if s == SLOTS - 1:
                        nc.scalar.activation(s_sb[:, PAST:PAST + TS], s_sb[:, PAST:PAST + TS], ACT.Exp, bias=st_nm[:, :],
                                             accum_out=st_sum[:, 8:9]).then_inc(act_e, 1)

                def sample_evac(b, s):
                    act.wait_ge(pe_t2, t2_at(b, ("s", s)) + 1)
                    act.wait_ge(pe_pv, b * PAGES + (4 * s - PAGES + VR))
                    nc.scalar.copy(pt_s[:, :, :].rearrange("p t q -> p (t q)"), b6[:, :]).then_inc(act_t2, 1)
                    if s == SLOTS - 1:
                        act.wait_ge(pe_t2, t2_at(b, ("n", s)) + 1)
                        nc.scalar.copy(pt_n[:, :], b6[0:TS, 0:P]).then_inc(act_t2, 1)

                def batch(b, sample):
                    for s in range(SLOTS):
                        if sample:
                            sample_exp(b, s)
                        k_evac(b, s, 0, 0)
                        k_evac(b, s, 0, 2)
                        prompt_exp(b, s, 0)
                        if sample:
                            sample_evac(b, s)
                        k_evac(b, s, 1, 0)
                        k_evac(b, s, 1, 2)
                        prompt_exp(b, s, 1)
                        prompt_evac(b, s, 0)
                        prompt_evac(b, s, 1)

                batch(0, False)
                with act.Fori(1, NB) as b:
                    batch(b, True)

                def final_norm_row(i, src, rows):
                    act.wait_ge(dve_y, i + 1)
                    nc.scalar.activation(jk2[0:rows, :], src, ACT.Square, accum_out=ss[0:rows, i:i + 1]).then_inc(act_y, 1)
                    act.wait_ge(dve_v, i + 1)
                    nc.scalar.activation(ss[0:rows, i:i + 1], ss[0:rows, i:i + 1], ACT.Sqrt).then_inc(act_r, 1)

                for i in range(TT):
                    if i < 4:
                        for s in (2 * i, 2 * i + 1):
                            sample_exp(NB, s)
                            sample_evac(NB, s)
                    final_norm_row(i, x1_t[i % 3][:, :], P)
                final_norm_row(TT, xs_c[:, :], TS)

            @attend.vector
            def _(dve):
                V = nc.vector
                N_CA, N_CV = 17, 4

                def k_evac(b, s, h, m):
                    dve.wait_ge(pe_kt, b * 64 + (8 * s + 4 * h + m + 1))
                    past(dve, pe_qk, b * 16 + (2 * s + h - 1))
                    V.tensor_copy(kt[h][:, 2 * m:2 * m + 2, :].rearrange("p a k -> p (a k)"), b5[:, :]).then_inc(dve_kt, 1)

                def prompt_max(b, s, h):
                    dve.wait_ge(pe_s, b * 16 + (2 * s + h + 1))
                    V.tensor_reduce(pp_nm[:, h:h + 1], ps_a[:, 0:P * (QBLOCKS[s] + 1)], AX, ALU.max, negate=True)\
                        .then_inc(dve_mx, 1)

                def prompt_norm(b, s, h):
                    dve.wait_ge(act_p, b * 16 + (2 * s + h + 1))
                    V.reciprocal(pp_r[:, h:h + 1], pp_l[:, h:h + 1]).then_inc(dve_ca, 1)
                    dve.wait_ge(dve_ca, b * N_CA + (2 * s + h + 1))
                    n = P * (QBLOCKS[s] + 1)
                    V.tensor_scalar(p_p[:, h, 0:n], p_p[:, h, 0:n], pp_r[:, h:h + 1], None, ALU.mult).then_inc(dve_pn, 1)

                def queries(b):
                    past(dve, pe_new, b)
                    for par in range(2):
                        for hh in range(2):
                            c = 8 * par + NQ * hh
                            last = V.tensor_copy(q_bd[64 * hh:64 * hh + 64, par::2, c:c + NQ],
                                                 q_s[64 * hh:64 * hh + 64, par::2, bass.ds(b * NQ, NQ)])
                    last.then_inc(dve_q, 1)

                def sample_scores(b, s):
                    dve.wait_ge(pe_qk, b * 16 + (2 * s + 2))
                    if s % 4 == 0:
                        dve.wait_ge(ld_d[s // 4], b * 64 + 64)
                    c = slice(512 * s, 512 * s + 512)
                    V.scalar_tensor_tensor(s_sb[:, c], b7[:, :], cq[:, bass.ds(b, 1)], d_sb[:, c], ALU.add, ALU.add)\
                        .then_inc(dve_s, 1)
                    dve.wait_ge(dve_s, b * 9 + (s + 1))
                    V.tensor_reduce(st_max[:, s:s + 1], s_sb[:, c], AX, ALU.max)

                def new_scores(b):
                    dve.wait_ge(pe_new, b + 1)
                    V.scalar_tensor_tensor(s_sb[:, PAST:PAST + TS], b5[:, 0:TS], cq[:, bass.ds(b, 1)],
                                           d_new[:, bass.ds(b, 1), :].rearrange("p o t -> p (o t)"), ALU.add, ALU.add)\
                        .then_inc(dve_s, 1)
                    dve.wait_ge(dve_s, b * 9 + 9)
                    V.tensor_reduce(st_max[:, 8:9], s_sb[:, PAST:PAST + TS], AX, ALU.max).then_inc(dve_ca, 1)
                    dve.wait_ge(dve_ca, b * N_CA + N_CA)

                def gate(b, s):
                    dve.wait_ge(pe_pvp, b * 16 + (2 * s + 2))
                    r = P * QBLOCKS[s]
                    z = z_t[:, bass.ds(b, 1), r:r + P].rearrange("p o t -> p (o t)")
                    V.tensor_tensor(z, z, ps_b[:, 512:512 + P], ALU.mult).then_inc(dve_op, 1)

                def sum_exp(b):
                    dve.wait_ge(act_e, b * 9)
                    V.tensor_reduce(st_l[:, 0:1], st_sum[:, :], AX, ALU.add).then_inc(dve_cv, 1)

                def sample_out(b):
                    dve.wait_ge(dve_cv, b * N_CV + (1 - N_CV))
                    V.reciprocal(st_l[:, 1:2], st_l[:, 0:1]).then_inc(dve_cv, 1)
                    dve.wait_ge(dve_cv, b * N_CV + (2 - N_CV))
                    V.tensor_scalar(hm_l[:, :], con[:, C_HM:C_HM + 4], st_l[:, 1:2], None, ALU.mult).then_inc(dve_cv, 1)
                    dve.wait_ge(dve_cv, b * N_CV + (3 - N_CV))
                    dve.wait_ge(pe_vo, b)
                    V.tensor_tensor(o_raw[:, :, :], ps_b[:, 0:256].rearrange("p (h d) -> p h d", d=HD),
                                    hm_l[:, :].unsqueeze(2).to_broadcast([P, 4, HD]), ALU.mult).then_inc(dve_cv, 1)
                    dve.wait_ge(dve_cv, b * N_CV)
                    dve.wait_ge(o_free, b)
                    V.tensor_reduce(o_n[:, :], o_raw[:, :, :].rearrange("p h d -> p d h"), AX, ALU.add).then_inc(dve_ov, 1)

                def batch(b, sample):
                    queries(b)
                    for s in range(SLOTS):
                        prompt_max(b, s, 0)
                        k_evac(b, s, 0, 1)
                        k_evac(b, s, 0, 3)
                        prompt_norm(b, s, 0)
                        prompt_max(b, s, 1)
                        k_evac(b, s, 1, 1)
                        k_evac(b, s, 1, 3)
                        prompt_norm(b, s, 1)
                        sample_scores(b, s)
                        if s == SLOTS - 1:
                            new_scores(b)
                            if sample:
                                sum_exp(b)
                            V.tensor_reduce(st_nm[:, :], st_max[:, :], AX, ALU.max, negate=True).then_inc(dve_nm, 1)
                        gate(b, s)
                    if sample:
                        sample_out(b)

                dve.sem_inc(dve_ov, 1)
                V.memset(d_sb[:, :], 0.0).then_inc(dve_d0, 1)
                batch(0, False)
                with dve.Fori(1, NB) as b:
                    batch(b, True)

                def final(i, dst, rows):
                    dve.wait_ge(act_y, i + 1)
                    V.tensor_scalar(ss[0:rows, i:i + 1], ss[0:rows, i:i + 1], 1.0 / DM, EPS, ALU.mult, ALU.add)\
                        .then_inc(dve_v, 1)
                    dve.wait_ge(act_r, i + 1)
                    V.reciprocal(ss[0:rows, i:i + 1], ss[0:rows, i:i + 1]).then_inc(dve_ce, 1)
                    dve.wait_ge(dve_ce, i + 1)
                    V.scalar_tensor_tensor(dst, dst, ss[0:rows, i:i + 1], fn_b[0:rows, :], ALU.mult, ALU.mult)\
                        .then_inc(dve_n, 1)

                dve.wait_ge(ld_fn, 16)
                for i in range(TT):
                    dve.wait_ge(pe_y, i + 1)
                    dve.wait_ge(ld_x1[i % 3], 16 * (i // 3 + 1))
                    V.tensor_tensor(x1_t[i % 3][:, :], x1_t[i % 3][:, :], ps_a[:, :], ALU.add).then_inc(dve_y, 1)
                    if i == 3:
                        sum_exp(NB)
                        sample_out(NB)
                    if i == 6:
                        dve.wait_ge(pe_sm, 1)
                        V.tensor_tensor(h_s[:, :, :], b4[:, 0:KT8 * TS].rearrange("p (k t) -> p k t", t=TS),
                                        z_t[:, :, SEQ:SEQ + TS], ALU.mult).then_inc(dve_sm, 1)
                    final(i, x1_t[i % 3][:, :], P)
                dve.wait_ge(pe_sm, 2)
                V.tensor_copy(xs_c[:, :], x_s[32:64, :])
                V.tensor_copy(sm_p[:, :], ps_b[:, :]).then_inc(dve_sm, 1)
                dve.wait_ge(dve_sm, 2)
                V.tensor_tensor(xs_c[:, :], xs_c[:, :], x_s[0:TS, :], ALU.add).then_inc(dve_sm, 1)
                dve.wait_ge(dve_sm, 3)
                dve.wait_ge(pe_sm, 3)
                V.tensor_tensor(xs_c[:, :], xs_c[:, :], ps_b[0:TS, :], ALU.add).then_inc(dve_y, 1)
                final(TT, xs_c[:, :], TS)


_INS = ["x_prompt", "x_sample", "state_pool", "cache_k", "cache_v", "cache_logf", "page_table", "norm_g",
        "w_in_pool", "pool_mix", "pool_scale", "w_out_pool", "w_in_attn", "b_forget", "w_out_attn", "final_norm"]
_OUTS = [(1, SEQ, DM), (NB, NQ, DM), (1, 1, CTX, PW), (1, NB, CTX, PW), (1, 1, SEQ, NH, HD), (1, 1, SEQ, NH, HD),
         (1, 1, SEQ, NH), (1, NB, NQ, NH, HD), (1, NB, NQ, NH, HD), (1, NB, NQ, NH)]


def kernel(**inputs):
    import concourse.bacc as bacc
    from concourse.bass_utils import run_bass_kernel_spmd as run

    nc = bacc.Bacc("TRN2", target_bir_lowering=False, num_devices=1)
    arrays = {f"in_{n}_dram": np.ascontiguousarray(inputs[n]) for n in _INS}
    arrays["in_consts_dram"] = constants()
    args = [nc.dram_tensor(n, a.shape, mybir.dt.from_np(a.dtype), kind="ExternalInput").ap()
            for n, a in arrays.items()]
    args += [nc.dram_tensor(f"out_{i}_dram", shape, F32, kind="ExternalOutput").ap()
             for i, shape in enumerate(_OUTS)]
    build(nc, *args)
    r = run(nc, [arrays], core_ids=[0])
    return tuple(r.results[0][f"out_{i}_dram"] for i in range(len(_OUTS)))
```

```python
from contextlib import ExitStack

import numpy as np

import concourse.bass as bass
from concourse import mybir

F32 = mybir.dt.float32
F32R = mybir.dt.float32r
BF16 = mybir.dt.bfloat16
I32 = mybir.dt.int32
ALU = mybir.AluOpType
ACT = mybir.ActivationFunctionType
AX = mybir.AxisListType.X

P = 128
DM = 1024
SEQ = 1024
NB, NQ = 8, 4
TS = NB * NQ
PW = 2048
WINDOWS = (2, 4, 8, 16)
NG = len(WINDOWS)
CTX = 15
NH, HD = 16, 64
PAGES, PAGE = 32, 128
PAST = PAGES * PAGE
KT8 = DM // P
TT = SEQ // P
EPS = 1e-6
NEG = -1e30
AUG = HD + 2
QSCALE = HD ** -0.5

PAD = 16
SEG = CTX + NQ
U_S = PAD + SEQ
UW = U_S + NB * SEG
GC = CTX + TS

C_ID, C_SUM4, C_SEL = 0, 128, 160
C_MQ, C_NEG, C_TRI = 288, 544, 800
C_CAUS, C_INV, C_HM = 928, 1056, 1072
C_END = 1076

QBLOCKS = (0, 7, 1, 6, 2, 5, 3, 4)


def constants():
    c = np.zeros((P, C_END), np.float32)
    r = np.arange(P)
    c[:, C_ID:C_ID + P] = np.eye(P)
    c[r, C_SUM4 + r % TS] = 1.0
    head = np.where(r % 32 < 16, 4 * (r // 32) + (r % 32) // 4, -1)
    for h in range(NH):
        c[h, C_SEL:C_SEL + P] = head == h
    tok = np.arange(TS)[None]
    for b in range(NB):
        last = (NQ * b + r % NQ)[:, None]
        c[:, C_MQ + TS * b:C_MQ + TS * (b + 1)] = tok == last
        seen = (tok >= NQ * b) & (tok <= last)
        c[:, C_NEG + TS * b:C_NEG + TS * (b + 1)] = np.where(seen, 0.0, NEG)
    c[:, C_TRI:C_TRI + P] = (r[:, None] > r[None]) & (r[:, None] // PAGES == r[None] // PAGES)
    c[:, C_CAUS:C_CAUS + P] = np.where(r[None] > r[:, None], NEG, 0.0)
    c[:, C_INV:C_INV + 16] = 1.0 / np.arange(1, 17, dtype=np.float32)
    for hh in range(4):
        c[:, C_HM + hh] = (r % 32) // 4 == hh
    return c


CHUNKS = [("u", 0), ("u", 1), ("u", 2), ("u", 3), ("z", 0), ("m", 0), ("z", 1), ("m", 1), ("z", 2),
          ("o", 0), ("o", 1), ("m", 2), ("z", 3), ("m", 3), ("o", 2), ("o", 3)]
NCH = len(CHUNKS)
C_L0 = NG * NCH
CR_W = 2
B7 = 13
B7_AT = {("st", 0): 0, ("u", 0): 1, ("u", 1): 2, ("u", 2): 3, ("u", 3): 4, ("z", 0): 5, ("m", 0): 6,
         ("z", 1): 7, ("m", 1): 8, ("z", 2): 9, ("m", 2): 10, ("z", 3): 11, ("m", 3): 12}


def before(kinds, n):
    return sum(CHUNKS[i][0] in kinds for i in range(n))


def build(nc, x_prompt, x_sample, state_pool, cache_k, cache_v, cache_logf, page_table, norm_g,
          w_in_pool, pool_mix, pool_scale, w_out_pool, w_in_attn, b_forget, w_out_attn, final_norm,
          consts, y_prompt, y_sample, pool_prompt, pool_sample, k_prompt, v_prompt, logf_prompt,
          k_sample, v_sample, logf_sample):
    n_phys = cache_k.shape[1]

    def internal(name, shape):
        return nc.dram_tensor(name, shape, F32, kind="Internal").ap()

    q_aug = internal("q_aug", (NH, AUG, SEQ))
    k_aug = internal("k_aug", (NH, AUG, SEQ))
    decay = internal("decay", (NB, NH, PAST))
    o_smp = internal("o_smp", (TS, DM))
    x1_scr = internal("x1_scr", (SEQ, DM))

    with ExitStack() as ctx:
        base = (nc.sbuf_base + 63) // 64 * 64
        at = [base]

        def place(name, shape, dt=F32, where=None):
            n = int(np.prod(shape[1:])) * (2 if dt == BF16 else 4)
            off = at[0] if where is None else where
            if where is None:
                at[0] = off + (n + 31) // 32 * 32
            return nc.alloc_sbuf_tensor_at(name, list(shape), dt, offset=off)

        def sem(name):
            return ctx.enter_context(nc.semaphore(name))

        con = place("con", [P, C_END])
        ident = con[:, C_ID:C_ID + P]
        sum4 = con[:, C_SUM4:C_SUM4 + TS]
        ident_b = place("ident_b", [P, P], BF16)
        caus_b = place("caus_b", [P, P], BF16)
        x_s = place("x_s", [64, DM])
        q_s = place("q_s", [P, KT8, TS])
        k_s = place("k_s", [P, KT8, TS])
        q_bd = place("q_bd", [P, KT8, 32])
        d_new = place("d_new", [P, NB, TS])
        cq = place("cq", [P, NB])
        ss = place("ss", [P, TT + 1])
        st_max = place("st_max", [P, 9])
        st_nm = place("st_nm", [P, 1])
        st_sum = place("st_sum", [P, 9])
        st_l = place("st_l", [P, 2])
        hm_l = place("hm_l", [P, 4])
        pp_nm = place("pp_nm", [P, 2])
        pp_l = place("pp_l", [P, 2])
        pp_r = place("pp_r", [P, 2])
        pt_sb = place("pt_sb", [1, NB * PAGES], I32)
        g_t = place("g_t", [P, 2, KT8])
        sc_t = place("sc_t", [P, PW // P])
        bf_t = place("bf_t", [NH, 1])
        h_s = place("h_s", [P, KT8, TS])
        at_in = at[0]
        st_in = place("st_in", [NB * CTX, 512])
        st_t = place("st_t", [P, 4, NB * CTX])
        g_in = place("g_in", [P, 4, GC])
        g_out = place("g_out", [GC, 512])
        p_s = place("p_s", [P, 4, TS])
        ym_s = place("ym_s", [P, TS])
        sz_s = place("sz_s", [P, TS])
        y_s = place("y_s", [P, 2, TS])
        at_px = at[0]
        px_sb = place("px_sb", [P, P])
        ks_st = place("ks_st", [P, TS])
        vs_st = place("vs_st", [P, TS])
        ones = place("ones", [P, P])
        idx = place("idx", [P, 2], I32)
        cr_sb = place("cr_sb", [P, TS])
        big = at[0]

        def big_at(n):
            return big + 4 * n

        h_hi = place("h_hi", [P, KT8, SEQ], F32R, big_at(0))
        h_lo = place("h_lo", [P, KT8, SEQ], F32R, big_at(8192))
        w_raw = [place(f"w_raw{i}", [P, 1024], F32, big_at(16384 + 1024 * i)) for i in range(2)]
        w_hi = [place(f"w_hi{i}", [P, 1024], F32R, big_at(18432 + 1024 * i)) for i in range(2)]
        w_lo = [place(f"w_lo{i}", [P, 1024], F32R, big_at(20480 + 1024 * i)) for i in range(2)]
        AT_PO, AT_Y, AT_U = 22528, 30720, 34816
        po_hi = place("po_hi", [P, 4, SEQ], F32R, big_at(AT_PO))
        po_lo = place("po_lo", [P, 4, SEQ], F32R, big_at(AT_PO + 4096))
        y_hi = place("y_hi", [P, 2, SEQ], F32R, big_at(AT_Y))
        y_lo = place("y_lo", [P, 2, SEQ], F32R, big_at(AT_Y + 2048))
        u_sb = place("u_sb", [P, UW], F32, big_at(AT_U))
        t1 = place("t1", [P, UW], F32, big_at(AT_U + UW))
        t2 = place("t2", [P, UW], F32, big_at(AT_U + 2 * UW))
        AT_X = AT_U + 3 * UW + 48
        x_p = place("x_p", [P, TT, DM], F32, big_at(AT_X))
        xn = place("xn", [P, TT, DM], F32, big_at(AT_PO))
        xn_s = place("xn_s", [TS, DM], F32, big_at(AT_Y))
        xt_s = place("xt_s", [TS, DM], F32, big_at(AT_Y + 1024))
        junk = place("junk", [P, DM], F32, big_at(AT_Y + 2048))
        q_st = place("q_st", [P, SEQ], F32, big_at(AT_PO))
        k_st = place("k_st", [P, SEQ], F32, big_at(AT_PO + 1024))
        v_st = place("v_st", [P, SEQ], F32, big_at(AT_PO + 2048))
        k_tm = place("k_tm", [P, TT, P], F32, big_at(AT_PO + 3072))
        v_tm = place("v_tm", [P, TT, P], F32, big_at(AT_PO + 4096))
        ks_tm = place("ks_tm", [TS, DM], F32, big_at(AT_PO + 5120))
        wf = place("wf", [P, KT8, P], F32, big_at(AT_Y + 3072))
        LW = SEQ + TS
        lf = [place(f"lf{i}", [NH, LW], F32, big_at(AT_PO + 6400 if i == 0 else AT_Y + LW * (i - 1)))
              for i in range(5)]
        lp = place("lp", [P, 2048], F32, big_at(AT_Y))
        pfx = [place(f"pfx{i}", [P, NH, PAGE], F32, big_at(AT_Y + 2048 * (i + 1))) for i in range(2)]
        tot = place("tot", [P, 2, NH], F32, big_at(AT_Y + 6144))
        lf_tm = place("lf_tm", [P, TT, NH], F32, big_at(AT_Y + 6176))
        lfs_tm = place("lfs_tm", [TS, NH], F32, big_at(AT_Y + 6304))
        c_s = place("c_s", [NH, TS], F32, big_at(AT_Y + 6320))
        mq_w = place("mq_w", [P, NB, TS], F32, big_at(AT_Y + 6352))
        z_t = place("z_t", [P, KT8, SEQ + TS], F32, big_at(AT_X))
        vs_tm = place("vs_tm", [TS, DM], F32, big_at(37408))
        o_raw = place("o_raw", [P, 4, HD], F32, at_in)
        o_n = place("o_n", [P, HD], F32, at_in + 1024)
        KR, VR = 8, 8
        k_pg = place("k_pg", [P, KR, DM], F32, big_at(0))
        v_pg = place("v_pg", [P, VR, DM], F32, big_at(8192))
        kt = [place(f"kt{i}", [P, KT8, 256], F32, big_at(16384 + 2048 * i)) for i in range(2)]
        s_sb = place("s_sb", [P, PAST + TS], F32, big_at(20480))
        d_sb = place("d_sb", [P, PAST], F32, big_at(24608))
        pt_s = place("pt_s", [P, 4, P], F32, big_at(28704))
        qa = place("qa", [AUG, 2, SEQ], F32, big_at(29216))
        ka = place("ka", [AUG, 2, SEQ], F32, big_at(31264))
        v_pr = place("v_pr", [P, TT, P], F32, big_at(33312))
        p_p = place("p_p", [P, 2, SEQ], F32, big_at(34336))
        pt_p = place("pt_p", [P, TT, P], F32, big_at(36384))
        w_o = place("w_o", [P, KT8, DM], F32, big_at(0))
        wo_lo = place("wo_lo", [P, KT8, DM], F32R, big_at(0))
        wo_hi = [place(f"wo_hi{k}", [P, DM], F32R, big_at(31264 + 1024 * k if k < 6 else 24608 + 1024 * (k - 6)))
                 for k in range(KT8)]
        z_hi = [place(f"z_hi{i}", [P, KT8, P], F32R, big_at(26656 + 1024 * i)) for i in range(2)]
        z_lo = place("z_lo", [P, KT8, SEQ + TS], F32R, big_at(AT_X))
        x1_t = [place(f"x1_t{i}", [P, DM], F32, big_at(16384 + 1024 * i)) for i in range(3)]
        fn_b = place("fn_b", [P, DM], F32, big_at(29216))
        jk2 = place("jk2", [P, DM], F32, big_at(30240))
        os_tm = place("os_tm", [TS, DM], F32, big_at(20480))
        assert big_at(AT_X + KT8 * (SEQ + TS)) <= nc.sbuf_usable_end, (big, nc.sbuf_usable_end)

        ps_a = ctx.enter_context(nc.psum_tensor("ps_a", [P, 1024], F32))
        ps_b = ctx.enter_context(nc.psum_tensor("ps_b", [P, 1024], F32))
        b4, b5, b6, b7 = (ctx.enter_context(nc.psum_tensor(f"b{i}", [P, 512], F32)) for i in range(4, 8))
        out_b = (b4, b5)
        turn_b = (b4[:, :], b5[:, :], ps_a[:, 0:512], ps_b[:, 0:512])

        ld_con, ld_rows, ld_small, ld_wf, ld_st = (sem(n) for n in ("ld_con", "ld_rows", "ld_small", "ld_wf", "ld_st"))
        ld_x = [sem(f"ld_x{i}") for i in range(TT + 1)]
        ld_w = [sem("ld_w0"), sem("ld_w1")]
        ld_lp = [sem("ld_lp0"), sem("ld_lp1")]
        spill, st_pool, st_aug, st_tm, st_lf, st_dec, st_dense = (
            sem(n) for n in ("spill", "st_pool", "st_aug", "st_tm", "st_lf", "st_dec", "st_dense"))
        pool_free, go_free, pool_held = sem("pool_free"), sem("go_free"), sem("pool_held")
        smp_used, tile_done, pe_b7, pe_o = sem("smp_used"), sem("tile_done"), sem("pe_b7"), sem("pe_o")
        pe_nt, pe_nts, pe_tm, pe_tail, pe_g, pe_gt, act_g = (
            sem(n) for n in ("pe_nt", "pe_nts", "pe_tm", "pe_tail", "pe_g", "pe_gt", "act_g"))
        act_hi, act_px, act_b7, act_u, act_z = (sem(n) for n in ("act_hi", "act_px", "act_b7", "act_u", "act_z"))
        act_ss, act_sq, act_nt, act_t, act_lf = (sem(n) for n in ("act_ss", "act_sq", "act_nt", "act_t", "act_lf"))
        dve_c, dve_lo, dve_px, dve_pool = sem("dve_c"), sem("dve_lo"), sem("dve_px"), sem("dve_pool")
        dve_m, dve_mf, dve_o, dve_xt = sem("dve_m"), sem("dve_mf"), sem("dve_o"), sem("dve_xt")
        dve_var, dve_xn, dve_nt, dve_nts = sem("dve_var"), sem("dve_xn"), sem("dve_nt"), sem("dve_nts")
        dve_dec = sem("dve_dec")
        dve_lf, dve_tm, dve_tot, dve_tail = sem("dve_lf"), sem("dve_tm"), sem("dve_tot"), sem("dve_tail")
        dve_cst, dve_wf = sem("dve_cst"), sem("dve_wf")

        PX_L0, B7_L0 = NG * 12, NG * B7


        def tile_ps(parity):
            return ps_b if parity else ps_a

        def past(eng, semaphore, n):
            if not isinstance(n, int) or n > 0:
                eng.wait_ge(semaphore, n)

        k_full = [sem(f"k_full{r}") for r in range(KR)]
        ld_qk, pe_kt = sem("ld_qk"), sem("pe_kt")

        def k_page(sp, b, p):
            page = sp.value_load(pt_sb[0:1, bass.ds(b * PAGES + p, 1)], min_val=0, max_val=n_phys - 1)
            past(sp, pe_kt, b * 64 + 4 * (p // 2 - 3))
            sp.dma_start(k_pg[:, p % KR, :], cache_k[0, bass.ds(page, 1)].rearrange("o k h d -> (o k) (h d)"))\
              .then_inc(k_full[p % KR], 16)

        def qk_pair(pool, b):
            for src, dst in ((q_aug, qa), (k_aug, ka)):
                pool.dma_start(dst[:, :, :], src[bass.ds(b * 2, 2), :, :].rearrange("h d t -> d h t"))\
                    .then_inc(ld_qk, 16)

        with nc.Block() as block:

            @block.sync
            def _(sp):
                sp.dma_start(px_sb[0:16, :], norm_g.rearrange("n (k p) -> (n k) p", p=P)).then_inc(ld_rows, 16)
                sp.dma_start(px_sb[16:32, :], pool_scale[0].rearrange("(k p) -> k p", p=P)).then_inc(ld_rows, 16)
                sp.dma_start(x_s[0:TS, :], x_sample.rearrange("b q d -> (b q) d")).then_inc(ld_x[TT], 16)
                for i in range(TT):
                    sp.dma_start(x_p[:, i, :], x_prompt[0, P * i:P * i + P, :]).then_inc(ld_x[i], 16)

                with sp.Fori(0, NG) as g:
                    sp.wait_ge(pe_b7, g * B7 + 1)
                    sp.dma_start(st_in[:, :], state_pool[0].rearrange("b t c -> (b t) c")[:, bass.ds(g * 512, 512)])\
                      .then_inc(ld_st, 16)
                    for n, (kind, i) in enumerate(CHUNKS):
                        sp.wait_ge(dve_lo, g * NCH + n + 1)
                        sp.wait_ge(smp_used, g * NCH + n + 1)
                        dst = w_raw[n % 2]
                        if kind in "uz":
                            col = g * 512 + ((PW if kind == "z" else 0) + 128 * i)
                            sp.dma_start(dst[:, :].rearrange("p (k n) -> p k n", n=P),
                                         w_in_pool[0].rearrange("(k p) c -> p k c", p=P)[:, :, bass.ds(col, P)])\
                              .then_inc(ld_w[n % 2], 16)
                        elif kind == "m":
                            sp.dma_start(dst[:, 0:512].rearrange("p (c n) -> p c n", n=P),
                                         pool_mix[0, bass.ds(g, 1), :, 128 * i:128 * i + 128]
                                         .rearrange("o (c p) n -> p (o c) n", p=P)).then_inc(ld_w[n % 2], 16)
                        else:
                            row = g * 512 + 256 * (i // 2)
                            half = i % 2
                            sp.dma_start(dst[:, :].rearrange("p (k n) -> p k n", n=512),
                                         w_out_pool[0, bass.ds(row, 256), 512 * half:512 * half + 512]
                                         .rearrange("(k p) n -> p k n", p=P)).then_inc(ld_w[n % 2], 16)

                sp.wait_ge(dve_o, 2 + NG * 32)
                sp.dma_start(x1_scr.rearrange("(t p) d -> p t d", p=P), x_p[:, :, :]).then_inc(spill, 16)
                sp.wait_ge(dve_wf, 1)
                sp.dma_start(wf[:, :, 0:NH], w_in_attn[0, :, 4 * DM:4 * DM + NH].rearrange("(k p) n -> p k n", p=P))\
                  .then_inc(ld_wf, 16)
                with sp.Fori(0, KT8) as f:
                    for n in range(4):
                        sp.wait_ge(dve_lo, f * 4 + (C_L0 + n + 2))
                        sp.wait_ge(smp_used, f * 4 + (C_L0 + n + 2))
                        sp.dma_start(w_raw[n % 2][:, :].rearrange("p (k n) -> p k n", n=P),
                                     w_in_attn[0].rearrange("(k p) c -> p k c", p=P)[:, :, bass.ds(f * P + n * DM, P)])\
                          .then_inc(ld_w[n % 2], 16)
                for t in range(2):
                    sp.wait_ge(dve_dec, t + 1)
                    for b in range(4):
                        sp.dma_start(decay[4 * t + b].rearrange("h (g k) -> g h k", k=PAGE),
                                     pfx[t][32 * b:32 * b + 32, :, :]).then_inc(st_dec, 16)
                sp.wait_ge(dve_tail, 1)
                sp.dma_start(logf_prompt[0, 0].rearrange("(t p) h -> p t h", p=P), lf_tm[:, :, :]).then_inc(st_dense, 16)
                sp.dma_start(logf_sample[0].rearrange("b q h -> (b q) h"), lfs_tm[:, :]).then_inc(st_dense, 16)
                sp.wait_ge(tile_done, C_L0 + 1 + 4 * KT8 + CR_W)
                for p in range(2):
                    k_page(sp, 0, p)
                sp.wait_ge(act_b7, 1 + B7_L0 + 1 + 6 * KT8)
                sp.dma_start(k_sample[0].rearrange("b q h d -> (b q) (h d)"), ks_tm[:, :]).then_inc(st_dense, 16)
                sp.dma_start(v_sample[0].rearrange("b q h d -> (b q) (h d)"), vs_tm[:, :]).then_inc(st_dense, 16)
                for p in range(2, KR):
                    k_page(sp, 0, p)
                sp.wait_ge(spill, 16)

            def hold(pool):
                pool.sem_inc(pool_held, 1)

            @block.gpsimd
            def _(pool):
                pool.sem_inc(go_free, 1)
                pool.sem_inc(pool_free, 1)
                pool.dma_start(pool_sample[0, :, 0:CTX - NQ, :], state_pool[0, :, NQ:CTX, :]).then_inc(st_pool, 16)
                with pool.Fori(0, NG) as g:
                    pool.wait_ge(act_g, g + 1)
                    hold(pool)
                    pool.dma_start(pool_prompt[0, 0, :, bass.ds(g * 512, 512)], g_out[0:CTX, :]).then_inc(st_pool, 16)
                    pool.dma_start(pool_sample[0].rearrange("b t c -> b t c")[:, CTX - NQ:CTX, bass.ds(g * 512, 512)],
                                   g_out[CTX:GC, :]).then_inc(st_pool, 16)
                    pool.wait_ge(st_pool, g * 32 + 48)
                    pool.sem_inc(go_free, 1)

                def stores(f):
                    pool.wait_ge(act_t, f * 4 + 3)
                    hold(pool)
                    for hh in range(2):
                        pool.dma_start(q_aug[bass.ds(f * 2 + hh, 1), 0:HD, :].rearrange("o d t -> d (o t)"),
                                       q_st[64 * hh:64 * hh + 64, :]).then_inc(st_aug, 16)
                    pool.wait_ge(act_t, f * 4 + 4)
                    hold(pool)
                    for hh in range(2):
                        pool.dma_start(k_aug[bass.ds(f * 2 + hh, 1), 0:HD, :].rearrange("o d t -> d (o t)"),
                                       k_st[64 * hh:64 * hh + 64, :]).then_inc(st_aug, 16)
                    pool.wait_ge(dve_tm, f * 4 + 4)
                    hold(pool)
                    pool.dma_start(k_prompt[0, 0].rearrange("(t p) h d -> p t (h d)", p=P)[:, :, bass.ds(f * P, P)],
                                   k_tm[:, :, :]).then_inc(st_tm, 16)
                    pool.wait_ge(dve_tm, f * 4 + 6)
                    hold(pool)
                    pool.dma_start(v_prompt[0, 0].rearrange("(t p) h d -> p t (h d)", p=P)[:, :, bass.ds(f * P, P)],
                                   v_tm[:, :, :]).then_inc(st_tm, 16)
                    pool.wait_ge(st_aug, f * 64 + 64)
                    pool.wait_ge(st_tm, f * 32 + 32)
                    pool.sem_inc(pool_free, 1)

                stores(0)
                pool.wait_ge(dve_lf, 6)
                for dst, src in ((q_aug[:, HD, :], lf[1]), (q_aug[:, HD + 1, :], lf[3]),
                                 (k_aug[:, HD, :], lf[3]), (k_aug[:, HD + 1, :], lf[2])):
                    pool.dma_start(dst, src[:, 0:SEQ]).then_inc(st_lf, 16)
                pool.wait_ge(st_lf, 64)
                for t, tiles in ((0, (1, 4)), (1, (4, KT8 - 1))):
                    if t:
                        pool.wait_ge(dve_tot, 1)
                    pool.indirect_dma_start(lp[:, :], None, cache_logf[0].rearrange("n k h -> n (k h)"),
                                            bass.IndirectOffsetOnAxis(ap=idx[:, t:t + 1], axis=0)).then_inc(ld_lp[t], 16)
                    with pool.Fori(*tiles) as f:
                        stores(f)
                pool.wait_ge(st_dec, 16 * 8)
                pool.wait_ge(dve_tail, 2)
                qk_pair(pool, 0)
                stores(KT8 - 1)

            @block.scalar
            def _(act):
                act.dma_start(con[:, :], consts).then_inc(ld_con, 16)
                act.dma_start(bf_t[:, :], b_forget[0].rearrange("(h o) -> h o", o=1)).then_inc(ld_small, 16)
                act.dma_start(pt_sb[:, :], page_table.rearrange("(o b) g -> o (b g)", o=1)).then_inc(ld_small, 16)
                act.dma_start(idx[:, :], page_table.rearrange("(t b) g -> (b g) t", t=2), allow_slow_non_contiguous=True)\
                    .then_inc(ld_small, 16)
                act.sem_inc(act_px, 1)
                act.sem_inc(act_b7, 1)
                act.sem_inc(act_z, 1)
                act.sem_inc(act_t, 1)

                def norm(n):
                    act.wait_ge(dve_cst, 1)
                    for half in range(2):
                        for i in range(4 * half, 4 * half + 4):
                            if n:
                                act.wait_ge(dve_o, 2 + NG * 32 - TT + i + 1)
                            else:
                                act.wait_ge(ld_x[i], 16)
                            last = nc.scalar.activation(xn[:, i, :], x_p[:, i, :], ACT.Square, accum_out=ss[:, i:i + 1])
                        if half:
                            act.wait_ge(dve_xt, n + 1)
                            last = nc.scalar.activation(junk[0:TS, :], xt_s[:, :], ACT.Square, accum_out=ss[0:TS, TT:TT + 1])
                        last.then_inc(act_ss, 1)
                        act.wait_ge(dve_var, 2 * n + half + 1)
                        c = slice(4, TT + 1) if half else slice(0, 4)
                        nc.scalar.activation(ss[:, c], ss[:, c], ACT.Sqrt).then_inc(act_sq, 1)
                    act.wait_ge(dve_cst, 2)
                    for f in range(16):
                        act.wait_ge(pe_nt, 16 * n + f + 1)
                        k, half = f % 8, f // 8
                        nc.scalar.activation(h_hi[:, k, 512 * half:512 * half + 512], turn_b[f % 4], ACT.Copy,
                                             scale=g_t[:, n, k:k + 1]).then_inc(act_nt, 1)

                def hi(c, slot, raw, width=1024):
                    act.wait_ge(tile_done, c + 1)
                    nc.scalar.copy(w_hi[slot][:, 0:width], raw[:, 0:width]).then_inc(act_hi, 1)

                def px(smp):
                    act.wait_ge(smp_used, smp)
                    nc.scalar.copy(px_sb[:, :], b6[:, 0:P]).then_inc(act_px, 1)

                def group(g, last):
                    act.wait_ge(pe_b7, g * B7 + (B7 + 1))
                    nc.scalar.copy(st_t[:, :, :].rearrange("p i r -> p (i r)"), b7[:, 0:480]).then_inc(act_b7, 1)
                    for n, (kind, i) in enumerate(CHUNKS):
                        if kind != "o":
                            px(g * NCH + (n + 1 + CR_W))
                        if n < NCH - 1:
                            act.wait_ge(ld_w[(n + 1) % 2], g * (8 * 16) + 16 * ((n + 1) // 2 + 1))
                            hi(g * NCH + (n + 1), (n + 1) % 2, w_raw[(n + 1) % 2], 512 if CHUNKS[n + 1][0] == "m" else 1024)
                        elif not last:
                            act.wait_ge(ld_w[0], g * (8 * 16) + (8 * 16 + 16))
                            hi(g * NCH + NCH, 0, w_raw[0])
                        ps = tile_ps((before("uzm", n)) % 2)
                        b7_at = g * B7 + (B7 + B7_AT.get((kind, i), 0) + 1)
                        if kind == "u":
                            act.wait_ge(tile_done, g * NCH + (n + 1 + CR_W))
                            act.wait_ge(dve_pool, g * 4 + (i + 1))
                            segs = u_sb[:, U_S:UW].rearrange("p (b s) -> p b s", s=SEG)
                            act.wait_ge(act_b7, g * B7 + 2)
                            nc.scalar.copy(segs[:, :, 0:CTX], st_t[:, i, :].rearrange("p (b s) -> p b s", s=CTX))
                            act.wait_ge(pe_b7, b7_at)
                            nc.scalar.copy(segs[:, :, CTX:SEG], b7[:, 0:TS].rearrange("p (b s) -> p b s", s=NQ))
                            nc.scalar.copy(g_in[:, i, CTX:GC], b7[:, 0:TS]).then_inc(act_b7, 1)
                            nc.scalar.copy(u_sb[:, PAD:U_S], ps[:, :])
                            nc.scalar.copy(g_in[:, i, 0:CTX], ps[:, SEQ - CTX:SEQ]).then_inc(act_u, 1)
                        if kind == "z":
                            act.wait_ge(tile_done, g * NCH + (n + 1 + CR_W))
                            act.wait_ge(dve_m, g * 8 + (2 * i + 1))
                            if i == 0:
                                act.wait_ge(dve_pool, g * 4 + 5)
                            act.wait_ge(pe_b7, b7_at)
                            nc.scalar.activation(sz_s[:, :], b7[:, 0:TS], ACT.Silu).then_inc(act_b7, 1)
                            nc.scalar.activation(t2[:, 0:SEQ], ps[:, :], ACT.Silu).then_inc(act_z, 1)
                        if kind == "m":
                            act.wait_ge(pe_b7, b7_at)
                            nc.scalar.activation(ym_s[:, :], b7[:, 0:TS], ACT.Copy,
                                                 scale=sc_t[:, bass.ds(g * 4 + i, 1)]).then_inc(act_b7, 1)
                            if i == 0:
                                act.wait_ge(pe_gt, g + 1)
                                act.wait_ge(go_free, g + 1)
                                nc.scalar.copy(g_out[:, :], b4[0:GC, :]).then_inc(act_g, 1)

                norm(0)
                act.wait_ge(ld_small, 48)
                act.wait_ge(ld_w[0], 16)
                hi(0, 0, w_raw[0])
                with act.Fori(0, NG - 1) as g:
                    group(g, False)
                group(NG - 1, True)
                norm(1)

                act.wait_ge(ld_wf, 16)
                hi(C_L0, 0, wf[:, :, :].rearrange("p k n -> p (k n)"))
                px(C_L0 + 1 + CR_W)
                act.wait_ge(ld_w[0], 16 * 33)
                hi(C_L0 + 1, 1, w_raw[0])
                px(C_L0 + 2 + CR_W)
                act.wait_ge(ld_w[1], 16 * 33)
                hi(C_L0 + 2, 0, w_raw[1])
                act.wait_ge(tile_done, C_L0 + 1 + CR_W)
                nc.scalar.activation(lf[0][:, 0:SEQ], ps_a[0:NH, :], ACT.Identity, bias=bf_t[:, :]).then_inc(act_t, 1)
                act.wait_ge(pe_b7, B7 + B7_L0 + 1)
                nc.scalar.activation(lf[0][:, SEQ:LW], b7[0:NH, 0:TS], ACT.Identity, bias=bf_t[:, :]).then_inc(act_b7, 1)
                act.wait_ge(dve_lf, 1)
                nc.scalar.activation(lf[1][:, :], lf[1][:, :], ACT.Exp, scale=-1.0).then_inc(act_lf, 1)
                act.wait_ge(dve_lf, 2)
                nc.scalar.activation(lf[2][:, :], lf[2][:, :], ACT.Ln).then_inc(act_lf, 1)

                def proj(f, first, last):
                    for n in range(4):
                        ahead = first and n == 0
                        if not ahead:
                            px(f * 4 + (C_L0 + 2 + n + CR_W))
                        if not ahead and not (last and n == 3):
                            act.wait_ge(ld_w[(n + 1) % 2], f * 32 + 16 * (33 + (n + 1) // 2))
                            hi(f * 4 + (C_L0 + 2 + n), n % 2, w_raw[(n + 1) % 2])
                        ps = tile_ps((n + 1) % 2)
                        act.wait_ge(tile_done, f * 4 + (C_L0 + 2 + n + CR_W))
                        b7_at = f * 6 + (B7 + B7_L0 + 1 + (0, 1, 2, 4)[n] + 1)
                        if n < 3:
                            act.wait_ge(pool_free, f + 1)
                        if n == 0:
                            act.wait_ge(pe_b7, b7_at)
                            nc.scalar.mul(q_s[:, bass.ds(f, 1), :].rearrange("p o n -> p (o n)"), b7[:, 0:TS], QSCALE)\
                              .then_inc(act_b7, 1)
                            nc.scalar.mul(q_st[:, :], ps[:, :], QSCALE).then_inc(act_t, 1)
                        elif n == 1:
                            act.wait_ge(pe_b7, b7_at)
                            nc.scalar.copy(ks_st[:, :], b7[:, 0:TS])
                            nc.scalar.copy(k_s[:, bass.ds(f, 1), :].rearrange("p o n -> p (o n)"), b7[:, 0:TS])\
                              .then_inc(act_b7, 1)
                            nc.scalar.copy(k_st[:, :], ps[:, :]).then_inc(act_t, 1)
                        elif n == 2:
                            nc.scalar.copy(v_st[:, :], ps[:, :]).then_inc(act_t, 1)
                            act.wait_ge(pe_b7, b7_at)
                            nc.scalar.copy(vs_st[:, :], b7[:, 0:TS]).then_inc(act_b7, 1)
                            act.wait_ge(pe_b7, b7_at + 1)
                            nc.scalar.copy(ks_tm[:, bass.ds(f * P, P)], b7[0:TS, 0:P]).then_inc(act_b7, 1)
                        else:
                            act.wait_ge(spill, 16)
                            act.wait_ge(dve_xn, 18)
                            nc.scalar.activation(z_t[:, bass.ds(f, 1), 0:SEQ].rearrange("p o n -> p (o n)"), ps[:, :],
                                                 ACT.Silu).then_inc(act_t, 1)
                            act.wait_ge(pe_b7, b7_at)
                            nc.scalar.activation(z_t[:, bass.ds(f, 1), SEQ:SEQ + TS].rearrange("p o n -> p (o n)"),
                                                 b7[:, 0:TS], ACT.Silu).then_inc(act_b7, 1)
                            act.wait_ge(pe_b7, b7_at + 1)
                            nc.scalar.copy(vs_tm[:, bass.ds(f * P, P)], b7[0:TS, 0:P]).then_inc(act_b7, 1)

                proj(0, True, False)
                with act.Fori(1, KT8 - 1) as f:
                    proj(f, False, False)
                proj(KT8 - 1, False, True)

            @block.tensor
            def _(pe):
                pe.sem_inc(smp_used, CR_W)
                pe.sem_inc(tile_done, CR_W)
                pe.sem_inc(pe_b7, B7)
                pe.wait_ge(ld_con, 16)
                pe.wait_ge(ld_rows, 32)
                nc.tensor.transpose(b6[:, 0:32], px_sb[0:32, :], con[0:32, C_ID:C_ID + 32]).then_inc(pe_g, 1)

                def norm(n):
                    for f in range(16):
                        k, half = f % 8, f // 8
                        pe.wait_ge(dve_xn, 9 * n + 4 * (half + 1))
                        if 16 * n + f >= 4:
                            pe.wait_ge(dve_nt, 16 * n + f - 3)
                        for i in range(4):
                            mm = nc.tensor.transpose(turn_b[f % 4][:, P * i:P * i + P],
                                                     xn[:, 4 * half + i, P * k:P * k + P], ident)
                        mm.then_inc(pe_nt, 1)
                    pe.wait_ge(dve_xn, 9 * n + 9)
                    if n:
                        pe.wait_ge(dve_px, 1 + NG * 4)
                    for k in range(KT8):
                        mm = nc.tensor.transpose(b6[:, TS * k:TS * k + TS], xn_s[:, P * k:P * k + P], con[0:TS, C_ID:C_ID + TS])
                    mm.then_inc(pe_nts, 1)
                    pe.wait_ge(dve_nt, 16 * n + 16)
                    pe.wait_ge(dve_nts, n + 1)

                def three(ps, pairs):
                    last = len(pairs) - 1
                    for j, (ah, al, bh, bl) in enumerate(pairs):
                        nc.tensor.matmul(ps, ah, bh, start=j == 0, stop=False)
                        nc.tensor.matmul(ps, ah, bl, start=False, stop=False)
                        mm = nc.tensor.matmul(ps, al, bh, start=False, stop=j == last)
                    return mm

                def sample_tile(raw, acts, nk):
                    for k in range(nk):
                        q = k % 4
                        mm = nc.tensor.matmul(b6[32 * q:32 * q + TS, 0:P], acts[:, k, :], raw[:, P * k:P * k + P],
                                              start=k < 4, stop=k >= nk - 4, tile_position=(0, 32 * q))
                    mm.then_inc(smp_used, 1)

                def prompt_tile(ps, slot, hi, lo, nk):
                    for half in range(2):
                        c = slice(512 * half, 512 * half + 512)
                        mm = three(ps[:, c], [(w_hi[slot][:, P * k:P * k + P], w_lo[slot][:, P * k:P * k + P],
                                               hi[:, k, c], lo[:, k, c]) for k in range(nk)])
                    mm.then_inc(tile_done, 1)

                def add_parts():
                    nc.tensor.matmul(b7[:, 0:TS], px_sb[:, :], sum4, start=True, stop=True).then_inc(pe_b7, 1)

                norm(0)
                with pe.Fori(0, NG) as g:
                    pe.wait_ge(ld_st, g * 16 + 16)
                    pe.wait_ge(act_b7, g * B7 + 1)
                    for i in range(4):
                        mm = nc.tensor.transpose(b7[:, 120 * i:120 * i + 120], st_in[:, P * i:P * i + P],
                                                 con[0:120, C_ID:C_ID + 120])
                    mm.then_inc(pe_b7, 1)
                    for n, (kind, i) in enumerate(CHUNKS):
                        slot, raw = n % 2, w_raw[n % 2]
                        t = before("uzm", n)
                        pe.wait_ge(ld_w[slot], g * 128 + 16 * (n // 2 + 1))
                        pe.wait_ge(act_px, g * 12 + (t + 1))
                        pe.wait_ge(dve_px, g * 4 + (before("o", n) + 1))
                        if kind == "m":
                            pe.wait_ge(dve_pool, g * 4 + 5)
                            sample_tile(raw, p_s, 4)
                        elif kind == "o":
                            if i == 0:
                                pe.wait_ge(act_g, g + 1)
                            pe.wait_ge(dve_m, g * 8 + 4 * (i // 2 + 1))
                            for k in range(2):
                                mm = nc.tensor.matmul(b6[32 * k:32 * k + TS, :], y_s[:, k, :], raw[:, 512 * k:512 * k + 512],
                                                      start=True, stop=True, tile_position=(0, 32 * k))
                            mm.then_inc(smp_used, 1)
                        else:
                            sample_tile(raw, h_s, KT8)
                        pe.wait_ge(dve_lo, g * NCH + (n + 1 + CR_W))
                        if kind == "o":
                            for u in range(TT):
                                pe.wait_ge(dve_o, g * 32 + (8 * i + u + 1))
                                if u == TT // 2:
                                    pe.wait_ge(dve_m, g * 8 + (4 * (i // 2 + 1) + 1))
                                r = slice(P * u, P * u + P)
                                mm = three(out_b[u % 2][:, :], [(y_hi[:, k, r], y_lo[:, k, r],
                                                                 w_hi[slot][:, 512 * k:512 * k + 512],
                                                                 w_lo[slot][:, 512 * k:512 * k + 512]) for k in range(2)])
                                mm.then_inc(pe_o if u < TT - 1 else tile_done, 1)
                            continue
                        free = {0: (act_z, 1), 1: (dve_mf, 1), 2: (act_u, 1), 3: (act_u, 2), 4: (act_u, 3),
                                5: (act_u, 4), 6: (act_z, 2), 7: (dve_mf, 2), 8: (act_z, 3), 9: (dve_mf, 3),
                                10: (act_z, 4), 11: (dve_mf, 4)}[t]
                        pe.wait_ge(free[0], g * 4 + free[1])
                        if (kind, i) == ("m", 0):
                            pe.wait_ge(act_u, g * 4 + 4)
                            pe.wait_ge(dve_o, g * 32 + 2)
                        if kind == "m":
                            prompt_tile(tile_ps(t % 2), slot, po_hi, po_lo, 4)
                        else:
                            prompt_tile(tile_ps(t % 2), slot, h_hi, h_lo, KT8)
                        if (kind, i) == ("m", 0):
                            for j in range(4):
                                mm = nc.tensor.transpose(b4[0:GC, P * j:P * j + P], g_in[:, j, :], ident)
                            mm.then_inc(pe_gt, 1)
                        pe.wait_ge(act_px, g * 12 + (t + 2))
                        pe.wait_ge(act_b7, g * B7 + (1 + B7_AT[kind, i]))
                        add_parts()
                norm(1)

                pe.wait_ge(ld_wf, 16)
                sample_tile(wf[:, :, :].rearrange("p k n -> p (k n)"), h_s, KT8)
                pe.wait_ge(dve_lo, C_L0 + 1 + CR_W)
                prompt_tile(ps_a, 0, h_hi, h_lo, KT8)
                pe.wait_ge(act_px, 1 + PX_L0 + 1)
                add_parts()
                def forget_tail():
                    pe.wait_ge(dve_tot, 2)
                    pe.wait_ge(dve_lf, 7)
                    pe.wait_ge(dve_tm, 2 + 4 * (KT8 - 1))
                    for t in range(2):
                        nc.tensor.matmul(b5[:, 64 + NH * t:64 + NH * t + NH], con[:, C_TRI:C_TRI + P], tot[:, t, :],
                                         start=True, stop=True)
                    nc.tensor.matmul(b5[:, 0:TS], con[0:NH, C_SEL:C_SEL + P], c_s[:, :], start=True, stop=True)
                    for i in range(TT):
                        nc.tensor.transpose(b4[:, NH * i:NH * i + NH], lf[0][:, P * i:P * i + P], con[0:NH, C_ID:C_ID + NH])
                    nc.tensor.transpose(b4[0:TS, 256:256 + NH], lf[0][:, SEQ:LW], con[0:NH, C_ID:C_ID + NH])\
                        .then_inc(pe_tail, 1)

                def proj(f, last):
                    if last:
                        forget_tail()
                    for n in range(4):
                        b7_at = f * 6 + (1 + B7_L0 + 1 + (0, 1, 2, 4)[n])
                        pe.wait_ge(ld_w[n % 2], f * 32 + 16 * (33 + n // 2))
                        pe.wait_ge(act_px, f * 4 + (1 + PX_L0 + 1 + n))
                        sample_tile(w_raw[n % 2], h_s, KT8)
                        pe.wait_ge(dve_lo, f * 4 + (C_L0 + 2 + n + CR_W))
                        pe.wait_ge(act_t, f * 4 + (n + 1))
                        prompt_tile(tile_ps((n + 1) % 2), (n + 1) % 2, h_hi, h_lo, KT8)
                        pe.wait_ge(act_px, f * 4 + (1 + PX_L0 + 2 + n))
                        pe.wait_ge(act_b7, b7_at)
                        add_parts()
                        if n < 2:
                            continue
                        src, src_s = (k_st, ks_st) if n == 2 else (v_st, vs_st)
                        pe.wait_ge(act_t, f * 4 + (n + 2))
                        if last and n == 2:
                            pe.wait_ge(dve_tail, 2)
                        for j in range(2):
                            pe.wait_ge(dve_tm, f * 4 + (2 * (n - 2) + j + 1))
                            for i in range(4):
                                r = P * (4 * j + i)
                                mm = nc.tensor.transpose(out_b[j][:, P * i:P * i + P], src[:, r:r + P], ident)
                            mm.then_inc(pe_tm, 1)
                        pe.wait_ge(act_b7, b7_at + 1)
                        nc.tensor.transpose(b7[0:TS, 0:P], src_s[:, :], ident).then_inc(pe_b7, 1)

                with pe.Fori(0, KT8 - 1) as f:
                    proj(f, False)
                proj(KT8 - 1, True)

            @block.vector
            def _(dve):
                chain = [0]

                def link(ins):
                    chain[0] += 1
                    ins.then_inc(dve_c, 1)
                    dve.wait_ge(dve_c, chain[0])

                V = nc.vector
                for s_, n_ in ((dve_lo, CR_W), (dve_px, 1), (dve_pool, 1), (dve_m, 1), (dve_mf, 1), (dve_o, 2), (dve_tm, 2)):
                    dve.sem_inc(s_, n_)
                V.memset(ones[:, :], 1.0)
                V.memset(u_sb[:, 0:PAD], 0.0)
                V.memset(q_bd[:, :, :], 0.0)
                V.memset(x_s[32:64, :], 0.0)
                V.memset(ss[:, :], 1.0).then_inc(dve_cst, 1)
                dve.wait_ge(ld_con, 16)
                V.tensor_copy(ident_b[:, :], ident)
                V.tensor_copy(caus_b[:, :], con[:, C_CAUS:C_CAUS + P])
                dve.wait_ge(pe_g, 1)
                V.tensor_copy(g_t[:, :, :].rearrange("p n k -> p (n k)"), b6[:, 0:16])
                V.tensor_copy(sc_t[:, :], b6[:, 16:32]).then_inc(dve_cst, 1)
                dve.wait_ge(dve_cst, 2)

                def norm(n):
                    dve.wait_ge(ld_x[TT], 16)
                    link(V.tensor_copy(xn_s[:, :], x_s[32:64, :]))
                    V.tensor_tensor(xt_s[:, :], x_s[0:TS, :], xn_s[:, :], ALU.add).then_inc(dve_xt, 1)
                    for half in range(2):
                        c = slice(4, TT + 1) if half else slice(0, 4)
                        dve.wait_ge(act_ss, 2 * n + half + 1)
                        V.tensor_scalar(ss[:, c], ss[:, c], 1.0 / DM, EPS, ALU.mult, ALU.add).then_inc(dve_var, 1)
                        dve.wait_ge(act_sq, 2 * n + half + 1)
                        link(V.reciprocal(ss[:, c], ss[:, c]))
                        for i in range(4 * half, 4 * half + 4):
                            V.tensor_scalar(xn[:, i, :], x_p[:, i, :], ss[:, i:i + 1], None, ALU.mult).then_inc(dve_xn, 1)
                    V.tensor_scalar(xn_s[:, :], xt_s[:, :], ss[0:TS, TT:TT + 1], None, ALU.mult).then_inc(dve_xn, 1)
                    for f in range(16):
                        k, half = f % 8, f // 8
                        dve.wait_ge(act_nt, 16 * n + f + 1)
                        c = slice(512 * half, 512 * half + 512)
                        V.scalar_tensor_tensor(h_lo[:, k, c], turn_b[f % 4], g_t[:, n, k:k + 1],
                                               h_hi[:, k, c].bitcast(F32), ALU.mult, ALU.subtract).then_inc(dve_nt, 1)
                    dve.wait_ge(pe_nts, n + 1)
                    V.tensor_tensor(h_s[:, :, :], b6[:, 0:KT8 * TS].rearrange("p (k t) -> p k t", t=TS),
                                    g_t[:, n, :].unsqueeze(2).to_broadcast([P, KT8, TS]), ALU.mult).then_inc(dve_nts, 1)

                def lo(c, slot, raw, width=1024):
                    dve.wait_ge(act_hi, c + 1)
                    V.tensor_tensor(w_lo[slot][:, 0:width], raw[:, 0:width], w_hi[slot][:, 0:width].bitcast(F32),
                                    ALU.subtract).then_inc(dve_lo, 1)

                def pool_tile(g, i):
                    w = WINDOWS[g]
                    dve.wait_ge(act_u, 4 * g + i + 1)
                    dve.wait_ge(act_b7, 1 + B7 * g + 2 + i)
                    cur, nxt, d, first = u_sb, t1, 1, 1
                    while d < w:
                        link(V.tensor_tensor(nxt[:, first:UW], cur[:, first:UW], cur[:, first - d:UW - d], ALU.add))
                        cur, nxt = nxt, (t2 if nxt is t1 else t1)
                        d *= 2
                        first += d
                    link(V.scalar_tensor_tensor(nxt[:, PAD:UW], cur[:, PAD:UW], 1.0 / w, u_sb[:, PAD:UW], ALU.mult, ALU.subtract))
                    e = slice(PAD, PAD + w - 1)
                    link(V.tensor_tensor(nxt[:, e], cur[:, e], con[:, C_INV:C_INV + w - 1], ALU.mult))
                    link(V.tensor_tensor(nxt[:, e], nxt[:, e], u_sb[:, e], ALU.subtract))
                    link(V.tensor_copy(po_hi[:, i, :], nxt[:, PAD:U_S]))
                    V.tensor_copy(p_s[:, i, :].rearrange("p (b q) -> p b q", q=NQ),
                                  nxt[:, U_S:UW].rearrange("p (b s) -> p b s", s=SEG)[:, :, CTX:SEG])
                    link(V.tensor_tensor(po_lo[:, i, :], nxt[:, PAD:U_S], po_hi[:, i, :].bitcast(F32), ALU.subtract))
                    dve.sem_inc(dve_pool, 1)

                def mix_tile(g, n, d):
                    dve.wait_ge(tile_done, NCH * g + n + 1 + CR_W)
                    dve.wait_ge(act_z, 4 * g + d + 2)
                    ps = tile_ps(before("uzm", n) % 2)
                    for half in range(2):
                        c = slice(512 * half, 512 * half + 512)
                        product = V.scalar_tensor_tensor(t1[:, c], ps[:, c], sc_t[:, 4 * g + d:4 * g + d + 1], t2[:, c],
                                                         ALU.mult, ALU.mult)
                        if half:
                            product.then_inc(dve_mf, 1)
                            dve.wait_ge(dve_mf, 4 * g + d + 2)
                        else:
                            link(product)
                        link(V.tensor_copy(y_hi[:, d % 2, c], t1[:, c]))
                        low = V.tensor_tensor(y_lo[:, d % 2, c], t1[:, c], y_hi[:, d % 2, c].bitcast(F32), ALU.subtract)
                        if half:
                            low.then_inc(dve_m, 1)
                        else:
                            dve.wait_ge(act_b7, 1 + B7 * g + B7_AT["m", d] + 1)
                            V.tensor_tensor(y_s[:, d % 2, :], ym_s[:, :], sz_s[:, :], ALU.mult).then_inc(dve_m, 1)

                def out_piece(g, n, j):
                    c = NCH * g + n
                    half = slice(512 * (j % 2), 512 * (j % 2) + 512)
                    dve.wait_ge(smp_used, c + 1 + CR_W)
                    V.tensor_tensor(x_s[:, half], x_s[:, half], b6[0:64, :], ALU.add).then_inc(dve_px, 1)
                    for u in range(TT):
                        if u < TT - 1:
                            dve.wait_ge(pe_o, (4 * g + j) * (TT - 1) + u + 1)
                        else:
                            dve.wait_ge(tile_done, c + 1 + CR_W)
                        V.tensor_tensor(x_p[:, u, half], x_p[:, u, half], out_b[u % 2][:, :], ALU.add).then_inc(dve_o, 1)

                norm(0)
                lo(0, 0, w_raw[0])
                for g in range(NG):
                    for n, (kind, i) in enumerate(CHUNKS):
                        if n < NCH - 1 or g < NG - 1:
                            nxt = CHUNKS[(n + 1) % NCH][0]
                            lo(NCH * g + n + 1, (n + 1) % 2, w_raw[(n + 1) % 2], 512 if nxt == "m" else 1024)
                        if kind == "u":
                            pool_tile(g, i)
                        elif kind == "m":
                            mix_tile(g, n, i)
                        elif kind == "o":
                            out_piece(g, n, i)
                V.memset(wf[:, :, :], 0.0).then_inc(dve_wf, 1)
                norm(1)
                dve.wait_ge(ld_wf, 16)
                lo(C_L0, 0, wf[:, :, :].rearrange("p k n -> p (k n)"))
                lo(C_L0 + 1, 1, w_raw[0])

                A, B, C, D, M = lf

                def log_forget_start():
                    dve.wait_ge(act_t, 2)
                    dve.wait_ge(act_b7, 1 + B7_L0 + 1)
                    V.scalar_tensor_tensor(B[:, :], A[:, :], -1.0, A[:, :], ALU.mult, ALU.max).then_inc(dve_lf, 1)
                    dve.wait_ge(act_lf, 1)
                    link(V.tensor_scalar(C[:, :], B[:, :], 1.0, None, ALU.add))
                    link(V.tensor_scalar(D[:, :], C[:, :], -1.0, None, ALU.add))
                    link(V.tensor_scalar(M[:, :], D[:, :], 0.0, None, ALU.is_equal))
                    V.tensor_tensor(D[:, :], D[:, :], M[:, :], ALU.add).then_inc(dve_lf, 1)

                def log_forget():
                    dve.wait_ge(dve_lf, 2)
                    link(V.reciprocal(D[:, :], D[:, :]))
                    dve.wait_ge(act_lf, 2)
                    link(V.tensor_tensor(C[:, :], C[:, :], M[:, :], ALU.add))
                    link(V.tensor_tensor(C[:, :], C[:, :], D[:, :], ALU.mult))
                    link(V.tensor_tensor(B[:, :], B[:, :], C[:, :], ALU.mult))
                    V.scalar_tensor_tensor(A[:, :], A[:, :], 0.0, B[:, :], ALU.min, ALU.subtract).then_inc(dve_lf, 1)

                def log_forget_sums():
                    V.memset(D[:, 0:SEQ], 1.0).then_inc(dve_lf, 1)
                    dve.wait_ge(dve_lf, 4)
                    V.tensor_tensor_scan(B[:, 0:SEQ], D[:, 0:SEQ], A[:, 0:SEQ], 0.0, ALU.mult, ALU.add).then_inc(dve_lf, 1)
                    dve.wait_ge(dve_lf, 5)
                    V.tensor_scalar(C[:, 0:SEQ], B[:, 0:SEQ], -1.0, None, ALU.mult).then_inc(dve_lf, 1)
                    new = A[:, SEQ:LW].rearrange("p (b q) -> p b q", q=NQ)
                    run = c_s[:, :].rearrange("p (b q) -> p b q", q=NQ)
                    link(V.tensor_copy(c_s[:, :], A[:, SEQ:LW]))
                    for q in range(1, NQ):
                        link(V.tensor_tensor(run[:, :, q], run[:, :, q - 1], new[:, :, q], ALU.add))
                    dve.sem_inc(dve_lf, 1)

                def page_sums(t):
                    dve.wait_ge(ld_lp[t], 16)
                    by_head = lp[:, :].rearrange("p (k h) -> p k h", h=NH)
                    for h in range(NH):
                        last = V.tensor_tensor_scan(pfx[t][:, h, :], ones[:, :], by_head[:, :, h], 0.0, ALU.mult, ALU.add)
                    link(last)
                    V.tensor_copy(tot[:, t, :], pfx[t][:, :, PAGE - 1]).then_inc(dve_tot, 1)

                def forget_tail():
                    dve.wait_ge(pe_tail, 1)
                    link(V.tensor_tensor(tot[:, :, :].rearrange("p t h -> p (t h)"), tot[:, :, :].rearrange("p t h -> p (t h)"),
                                         b5[:, 64:64 + 2 * NH], ALU.add))
                    for t in range(2):
                        for h in range(NH):
                            last = V.tensor_scalar(pfx[t][:, h, :], pfx[t][:, h, :], -1.0, tot[:, t, h:h + 1], ALU.mult, ALU.add)
                        last.then_inc(dve_dec, 1)
                    V.tensor_copy(lf_tm[:, :, :].rearrange("p t h -> p (t h)"), b4[:, 0:TT * NH])
                    V.tensor_copy(lfs_tm[:, :], b4[0:TS, 256:256 + NH]).then_inc(dve_tail, 1)
                    link(V.tensor_copy(cr_sb[:, :], b5[:, 0:TS]))
                    cr_b = cr_sb[:, :].unsqueeze(1).to_broadcast([P, NB, TS])
                    link(V.tensor_tensor(mq_w[:, :, :], con[:, C_MQ:C_MQ + NB * TS].rearrange("p (b t) -> p b t", t=TS), cr_b, ALU.mult))
                    V.tensor_reduce(cq[:, :], mq_w[:, :, :], AX, ALU.add)
                    V.tensor_tensor(d_new[:, :, :], con[:, C_NEG:C_NEG + NB * TS].rearrange("p (b t) -> p b t", t=TS), cr_b,
                                    ALU.subtract).then_inc(dve_tail, 1)

                lo(C_L0 + 2, 0, w_raw[1])
                log_forget_start()
                for f in range(KT8):
                    if f == KT8 - 1:
                        forget_tail()
                    for n in range(4):
                        if f + n > 0 and (f < KT8 - 1 or n < 3):
                            lo(C_L0 + 2 + 4 * f + n, n % 2, w_raw[(n + 1) % 2])
                        if f == 0 and n == 0:
                            log_forget()
                        if f == 0 and n == 1:
                            log_forget_sums()
                        if n >= 2:
                            dve.wait_ge(pool_free, f + 1)
                            for j in range(2):
                                dve.wait_ge(pe_tm, 4 * f + 2 * (n - 2) + j + 1)
                                V.tensor_copy((k_tm, v_tm)[n - 2][:, 4 * j:4 * j + 4, :].rearrange("p t n -> p (t n)"),
                                              out_b[j][:, :]).then_inc(dve_tm, 1)
                    if f in (3, 5):
                        page_sums((f - 3) // 2)

        SLOTS = 8
        HALF = 2 * PAGE
        pt_n = place("pt_n", [TS, P], F32, at_px)
        sm_p = place("sm_p", [P, DM], F32, big_at(19456))
        xs_c = place("xs_c", [TS, DM], F32, big_at(21504))

        def score_columns(s):
            n = QBLOCKS[s] + 1
            first = P if n == 5 else 0
            return first, first + P * n

        def fills(s):
            n = QBLOCKS[s] + 1
            return [(a, min(e, n) - a) for a, e in ((0, 4), (4, 7), (7, 8)) if a < n]

        def t2_uses(prompt, sample):
            uses = []
            for s in range(SLOTS):
                if sample:
                    uses.append(("s", s))
                    if s == SLOTS - 1:
                        uses.append(("n", s))
                if prompt:
                    for h in range(2):
                        uses += [(h, s, f) for f in range(len(fills(s)))]
            return uses

        y_ps = ((ps_a[:, 0:512], ps_a[:, 512:DM]), (b5[:, :], b7[:, :]))
        T2_FIRST, T2_BOTH, T2_LAST = t2_uses(True, False), t2_uses(True, True), t2_uses(False, True)

        def t2_at(b, key):
            if isinstance(b, int) and b == 0:
                return T2_FIRST.index(key)
            if isinstance(b, int) and b == NB:
                return len(T2_FIRST) + (NB - 1) * len(T2_BOTH) + T2_LAST.index(key)
            return b * len(T2_BOTH) + (len(T2_FIRST) - len(T2_BOTH) + T2_BOTH.index(key))

        def in_bank_3(key):
            return len(key) == 3 and key[2] == 1

        def t2_bank(key):
            return ps_b[:, 512 + P:1024] if in_bank_3(key) else b6[:, :]

        def t2_free(b, key):
            uses = T2_FIRST if isinstance(b, int) and b == 0 else T2_LAST if isinstance(b, int) else T2_BOTH
            i = uses.index(key)
            same = [j for j in range(i) if in_bank_3(uses[j]) == in_bank_3(key)]
            return t2_at(b, uses[0]) + (same[-1] + 1 if same else 0)

        v_full = [sem(f"v_full{r}") for r in range(VR)]
        ld_v, ld_os, ld_fn, st_o, st_y, o_free = (
            sem(n) for n in ("ld_v", "ld_os", "ld_fn", "st_o", "st_y", "o_free"))
        ld_d = [sem("ld_d0"), sem("ld_d1")]
        ld_x1 = [sem(f"ld_res{i}") for i in range(3)]
        pe_s, pe_t2, pe_qk, pe_new = (sem(n) for n in ("pe_s", "pe_t2", "pe_qk", "pe_new"))
        pe_pvp, pe_pv, pe_vo, pe_y, pe_sm = (sem(n) for n in ("pe_pvp", "pe_pv", "pe_vo", "pe_y", "pe_sm"))
        act_kt, act_p, act_t2, act_e, act_y, act_r = (
            sem(n) for n in ("act_kt", "act_p", "act_t2", "act_e", "act_y", "act_r"))
        dve_kt, dve_mx, dve_pn, dve_s, dve_op = (sem(n) for n in ("dve_kt", "dve_mx", "dve_pn", "dve_s", "dve_op"))
        dve_q, dve_nm, dve_ov, dve_d0, dve_y = (sem(n) for n in ("dve_q", "dve_nm", "dve_ov", "dve_d0", "dve_y"))
        dve_v, dve_n, dve_sm, dve_ca, dve_cv, dve_ce = (
            sem(n) for n in ("dve_v", "dve_n", "dve_sm", "dve_ca", "dve_cv", "dve_ce"))

        act_wh, dve_wl, act_zh, dve_zl = (sem(n) for n in ("act_wh", "dve_wl", "act_zh", "dve_zl"))

        with nc.Block() as attend:

            @attend.sync
            def _(sp):
                def v_page(b, p):
                    page = sp.value_load(pt_sb[0:1, bass.ds(b * PAGES + (p - PAGES), 1)], min_val=0, max_val=n_phys - 1)
                    sp.wait_ge(pe_pv, b * PAGES + (p - PAGES + 1))
                    sp.dma_start(v_pg[:, p % VR, :], cache_v[0, bass.ds(page, 1)].rearrange("o k h d -> (o k) (h d)"))\
                      .then_inc(v_full[p % VR], 16)

                for p in range(KR, PAGES):
                    k_page(sp, 0, p)
                with sp.Fori(1, NB) as b:
                    for p in range(PAGES):
                        k_page(sp, b, p)
                        v_page(b, p)
                for p in range(PAGES):
                    v_page(NB, p)
                    if p == 3:
                        sp.wait_ge(pe_kt, NB * 64)
                        for k in range(KT8):
                            sp.dma_start(w_o[:, k, :], w_out_attn[0, P * k:P * k + P, :]).then_inc(k_full[k], 16)
                sp.wait_ge(st_y, 16 * (TT + 1))

            @attend.gpsimd
            def _(pool):
                def decay_half(b, half):
                    c = slice(half * (PAST // 2), (half + 1) * (PAST // 2))
                    for j in range(4):
                        src = decay[bass.ds(b, 1), 4 * j:4 * j + 4, c].rearrange("o h c -> (o h) c")
                        pool.dma_start(d_sb[32 * j:32 * j + 16, c],
                                       src.unsqueeze(1).to_broadcast([4, NQ, PAST // 2])).then_inc(ld_d[half], 16)

                def v_pair(b):
                    pool.dma_start(v_pr[:, :, :], v_prompt[0, 0].rearrange("(t p) h d -> p t (h d)", p=P)
                                   [:, :, bass.ds(b * P, P)]).then_inc(ld_v, 16)

                def following(b):
                    pool.wait_ge(dve_s, b * 9 + 4)
                    hold(pool)
                    decay_half(b + 1, 0)
                    pool.wait_ge(pe_s, b * 16 + 16)
                    hold(pool)
                    qk_pair(pool, b + 1)
                    pool.wait_ge(pe_pvp, b * 16 + 16)
                    hold(pool)
                    v_pair(b + 1)
                    pool.wait_ge(dve_s, b * 9 + 8)
                    hold(pool)
                    decay_half(b + 1, 1)

                def sample_out(b):
                    pool.wait_ge(dve_ov, b + 1)
                    hold(pool)
                    for j in range(4):
                        pool.dma_start(o_smp[bass.ds(b * NQ - NQ, NQ), 256 * j:256 * j + 256]
                                       .rearrange("q (h d) -> h q d", d=HD),
                                       o_n[32 * j:32 * j + 16, :]).then_inc(st_o, 16)
                    pool.wait_ge(st_o, b * 64)
                    pool.sem_inc(o_free, 1)

                pool.sem_inc(o_free, 1)
                v_pair(0)
                pool.wait_ge(dve_d0, 1)
                decay_half(0, 0)
                decay_half(0, 1)
                following(0)
                with pool.Fori(1, NB - 1) as b:
                    following(b)
                    sample_out(b)
                pool.wait_ge(pe_s, NB * 16)
                pool.dma_start(fn_b[:, :], final_norm.unsqueeze(0).to_broadcast([P, DM])).then_inc(ld_fn, 16)
                pool.wait_ge(pe_new, NB)
                for i in range(3):
                    pool.dma_start(x1_t[i][:, :], x1_scr[P * i:P * i + P, :]).then_inc(ld_x1[i], 16)
                sample_out(NB - 1)
                for i in range(TT):
                    if i == 3:
                        sample_out(NB)
                        pool.wait_ge(st_o, 64 * NB)
                        pool.dma_start(os_tm[:, :], o_smp[:, :]).then_inc(ld_os, 16)
                    if i == TT - 1:
                        pool.wait_ge(dve_n, TT)
                        pool.dma_start(y_sample.rearrange("b q d -> (b q) d"), xs_c[:, :]).then_inc(st_y, 16)
                    pool.wait_ge(dve_n, i + 1 + (i == TT - 1))
                    pool.dma_start(y_prompt[0, P * i:P * i + P, :], x1_t[i % 3][:, :]).then_inc(st_y, 16)
                    if i + 3 < TT:
                        pool.wait_ge(st_y, 16 * (i + 1))
                        r = P * (i + 3)
                        pool.dma_start(x1_t[i % 3][:, :], x1_scr[r:r + P, :]).then_inc(ld_x1[i % 3], 16)

            @attend.tensor
            def _(pe):
                def scores(b, s, h):
                    qb = QBLOCKS[s]
                    if s == 0 and h == 0:
                        pe.wait_ge(ld_qk, b * 32 + 32)
                    past(pe, act_p, b * 16 + (2 * s + h))
                    first, last = score_columns(s)
                    for c, end in ((first, min(last, 512)), (512, last)):
                        if c < end:
                            nc.tensor.matmul(ps_a[:, c:end], qa[:, h, P * qb:P * qb + P], ka[:, h, c - first:end - first],
                                             start=True, stop=end < last)
                    nc.tensor.matmul(ps_a[:, last - P:last], ident_b[:, :], caus_b[:, :], start=False, stop=True)\
                        .then_inc(pe_s, 1)

                def k_turn(b, s, h, pairs):
                    p = 4 * s + 2 * h
                    for m in pairs:
                        if m == 0:
                            for i in range(2):
                                pe.wait_ge(k_full[(p + i) % KR], b * 64 + 16 * ((p + i) // KR + 1))
                        bank, free = ((b4, act_kt), (b5, dve_kt))[m % 2]
                        if s == 0 and h == 0 and m == 1:
                            past(pe, dve_s, b * 9)
                        past(pe, free, b * 32 + (4 * s + 2 * h + m // 2))
                        for j in range(2):
                            for i in range(2):
                                c = HALF * j + PAGE * i
                                f = P * (2 * m + j)
                                mm = nc.tensor.transpose(bank[:, c:c + PAGE], k_pg[:, (p + i) % KR, f:f + P], ident)
                        mm.then_inc(pe_kt, 1)

                def sample_scores(b, s, h, pairs):
                    if h == 0 and pairs[0] == 0:
                        past(pe, dve_s, b * 9 + s)
                    if h == 0 and s == 0:
                        pe.wait_ge(dve_q, b + 1)
                    pe.wait_ge(act_kt, b * 32 + (4 * s + 2 * h + 2))
                    pe.wait_ge(dve_kt, b * 32 + (4 * s + 2 * h + 2))
                    for pr in pairs:
                        r = 32 * (pr // 2)
                        mm = nc.tensor.matmul(b7[r:r + 32, HALF * h:HALF * h + HALF], q_bd[:, pr, :], kt[h][:, pr, :],
                                              start=pr % 2 == 0, stop=pr % 2 == 1, tile_position=(0, r))
                    if pairs[-1] == KT8 - 1:
                        mm.then_inc(pe_qk, 1)

                def new_scores(b):
                    pe.wait_ge(dve_kt, b * 32 + 32)
                    for pr in range(KT8):
                        r = 32 * (pr // 2)
                        mm = nc.tensor.matmul(b5[r:r + 32, 0:TS], q_bd[:, pr, :], k_s[:, pr, :],
                                              start=pr % 2 == 0, stop=pr % 2 == 1, tile_position=(0, r))
                    mm.then_inc(pe_new, 1)

                def prompt_turn(b, s, h, f):
                    if f == 0:
                        pe.wait_ge(dve_pn, b * 16 + (2 * s + h + 1))
                    if f < len(fills(s)):
                        past(pe, act_t2, t2_free(b, (h, s, f)))
                        if h == 0 and f == 1:
                            past(pe, dve_op, b * SLOTS + s)
                        for i in range(fills(s)[f][1]):
                            c = P * (fills(s)[f][0] + i)
                            mm = nc.tensor.transpose(t2_bank((h, s, f))[:, P * i:P * i + P], p_p[:, h, c:c + P], ident)
                        mm.then_inc(pe_t2, 1)

                def prompt_values(b, s, h):
                    if s == 0 and h == 0:
                        pe.wait_ge(ld_v, b * 16 + 16)
                    if h == 0:
                        past(pe, dve_op, b * SLOTS + s)
                    qb = QBLOCKS[s]
                    pe.wait_ge(act_t2, t2_at(b, (h, s, len(fills(s)) - 1)) + 1)
                    r = HD * h
                    for k in range(qb + 1):
                        mm = nc.tensor.matmul(ps_b[r:r + HD, 512:512 + P], v_pr[:, k, r:r + HD], pt_p[:, k, :],
                                              start=k == 0, stop=k == qb, tile_position=(0, r))
                    mm.then_inc(pe_pvp, 1)

                def sample_turn(b, s):
                    pe.wait_ge(act_e, b * 9 + (s + 1 - 9))
                    past(pe, act_t2, t2_free(b, ("s", s)))
                    for i in range(4):
                        c = PAGE * (4 * s + i)
                        mm = nc.tensor.transpose(t2_bank(("s", s))[:, P * i:P * i + P], s_sb[:, c:c + PAGE], ident)
                    mm.then_inc(pe_t2, 1)

                def new_turn(b):
                    pe.wait_ge(act_e, b * 9)
                    pe.wait_ge(act_t2, t2_free(b, ("n", SLOTS - 1)))
                    nc.tensor.transpose(b6[0:TS, 0:P], s_sb[:, PAST:PAST + TS], ident).then_inc(pe_t2, 1)

                def sample_values(b, s, pages):
                    new = s == SLOTS - 1 and pages[-1] == 3
                    pe.wait_ge(act_t2, t2_at(b, ("n" if new else "s", s)) + 1)
                    if s == 0 and pages[0] == 0:
                        pe.wait_ge(dve_ov, b)
                    for i in pages:
                        p = 4 * s + i
                        pe.wait_ge(v_full[p % VR], b * 64 + (16 * (p // VR + 1) - 64))
                        for j in range(4):
                            mm = nc.tensor.matmul(ps_b[32 * j:32 * j + 32, 0:256], pt_s[:, i, 32 * j:32 * j + 32],
                                                  v_pg[:, p % VR, 256 * j:256 * j + 256],
                                                  start=p == 0, stop=False, tile_position=(0, 32 * j))
                        mm.then_inc(pe_pv, 1)
                    if new:
                        for j in range(4):
                            mm = nc.tensor.matmul(ps_b[32 * j:32 * j + 32, 0:256], pt_n[:, 32 * j:32 * j + 32],
                                                  vs_tm[:, 256 * j:256 * j + 256],
                                                  start=False, stop=True, tile_position=(0, 32 * j))
                        mm.then_inc(pe_vo, 1)

                def batch(b, sample):
                    for s in range(SLOTS):
                        if s > 0:
                            prompt_values(b, s - 1, 1)
                        k_turn(b, s, 0, (0, 1))
                        if s == 0:
                            scores(b, 0, 0)
                        if sample:
                            sample_turn(b, s)
                        k_turn(b, s, 0, (2, 3))
                        if sample:
                            if s == SLOTS - 1:
                                new_turn(b)
                            sample_values(b, s, (0, 1))
                        scores(b, s, 1)
                        k_turn(b, s, 1, (0, 1))
                        sample_scores(b, s, 0, range(KT8))
                        k_turn(b, s, 1, (2,))
                        prompt_turn(b, s, 0, 0)
                        prompt_turn(b, s, 0, 1)
                        k_turn(b, s, 1, (3,))
                        prompt_turn(b, s, 0, 2)
                        if sample:
                            sample_values(b, s, (2, 3))
                        prompt_values(b, s, 0)
                        prompt_turn(b, s, 1, 0)
                        prompt_turn(b, s, 1, 1)
                        sample_scores(b, s, 1, range(4))
                        prompt_turn(b, s, 1, 2)
                        sample_scores(b, s, 1, range(4, KT8))
                        if s < SLOTS - 1:
                            scores(b, s + 1, 0)
                    new_scores(b)
                    prompt_values(b, SLOTS - 1, 1)

                pe.sem_inc(pe_pv, VR)
                batch(0, False)
                with pe.Fori(1, NB) as b:
                    batch(b, True)
                for i in range(TT):
                    if i == 0:
                        pe.wait_ge(dve_op, NB * SLOTS)
                    if i >= 2:
                        pe.wait_ge(dve_y, i - 1)
                    for part in range(2):
                        if i < 4:
                            sample_turn(NB, 2 * i + part)
                        for k in range(4 * part, 4 * part + 4):
                            if i == 0:
                                pe.wait_ge(dve_wl, k + 1)
                            if k == 0:
                                pe.wait_ge(dve_zl, i + 1)
                            high, low = z_hi[i % 2][:, k, :], z_lo[:, k, P * i:P * i + P]
                            for half in range(2):
                                c = slice(512 * half, 512 * half + 512)
                                out = y_ps[i % 2][half]
                                nc.tensor.matmul(out, high, wo_hi[k][:, c], start=k == 0, stop=False)
                                nc.tensor.matmul(out, high, wo_lo[:, k, c], start=False, stop=False)
                                mm = nc.tensor.matmul(out, low, wo_hi[k][:, c], start=False, stop=k == KT8 - 1)
                            if i == 3 and part and k == 5:
                                new_turn(NB)
                        if part:
                            mm.then_inc(pe_y, 1)
                        if i < 4:
                            sample_values(NB, 2 * i + part, range(4))
                    if i == 4:
                        pe.wait_ge(ld_os, 16)
                        for k in range(KT8):
                            mm = nc.tensor.transpose(b4[:, TS * k:TS * k + TS], os_tm[:, P * k:P * k + P],
                                                     con[0:TS, C_ID:C_ID + TS])
                        mm.then_inc(pe_sm, 1)
                    if i == 5:
                        pe.wait_ge(dve_sm, 1)
                        pe.wait_ge(dve_ov, NB + 1)
                        for half in range(2):
                            c = slice(512 * half, 512 * half + 512)
                            for k in range(KT8):
                                r = 32 * (k % 4)
                                nc.tensor.matmul(ps_b[r:r + TS, c], h_s[:, k, :], wo_hi[k][:, c].bitcast(F32),
                                                 start=k < 4, stop=False, tile_position=(0, r))
                                mm = nc.tensor.matmul(ps_b[r:r + TS, c], h_s[:, k, :], wo_lo[:, k, c].bitcast(F32),
                                                      start=False, stop=k >= 4, tile_position=(0, r))
                        mm.then_inc(pe_sm, 1)
                    if i == 6:
                        pe.wait_ge(dve_sm, 2)
                        for half in range(2):
                            c = slice(512 * half, 512 * half + 512)
                            mm = nc.tensor.matmul(ps_b[0:TS, c], sum4, sm_p[:, c], start=True, stop=True)
                        mm.then_inc(pe_sm, 1)

            @attend.scalar
            def _(act):
                def k_evac(b, s, h, m):
                    act.wait_ge(pe_kt, b * 64 + (8 * s + 4 * h + m + 1))
                    past(act, pe_qk, b * 16 + (2 * s + h - 1))
                    nc.scalar.copy(kt[h][:, 2 * m:2 * m + 2, :].rearrange("p a k -> p (a k)"), b4[:, :]).then_inc(act_kt, 1)

                def prompt_exp(b, s, h):
                    act.wait_ge(dve_mx, b * 16 + (2 * s + h + 1))
                    first, last = score_columns(s)
                    nc.scalar.activation(p_p[:, h, 0:last - first], ps_a[:, first:last], ACT.Exp, bias=pp_nm[:, h:h + 1],
                                         accum_out=pp_l[:, h:h + 1]).then_inc(act_p, 1)

                def prompt_evac(b, s, h):
                    for f, (first, n) in enumerate(fills(s)):
                        act.wait_ge(pe_t2, t2_at(b, (h, s, f)) + 1)
                        past(act, pe_pvp, b * 16 + (2 * s + h))
                        nc.scalar.copy(pt_p[:, first:first + n, :].rearrange("p t q -> p (t q)"), t2_bank((h, s, f))[:, 0:P * n])\
                            .then_inc(act_t2, 1)

                def sample_exp(b, s):
                    act.wait_ge(dve_nm, b)
                    c = slice(512 * s, 512 * s + 512)
                    nc.scalar.activation(s_sb[:, c], s_sb[:, c], ACT.Exp, bias=st_nm[:, :],
                                         accum_out=st_sum[:, s:s + 1]).then_inc(act_e, 1)
                    if s == SLOTS - 1:
                        nc.scalar.activation(s_sb[:, PAST:PAST + TS], s_sb[:, PAST:PAST + TS], ACT.Exp, bias=st_nm[:, :],
                                             accum_out=st_sum[:, 8:9]).then_inc(act_e, 1)

                def sample_evac(b, s):
                    act.wait_ge(pe_t2, t2_at(b, ("s", s)) + 1)
                    act.wait_ge(pe_pv, b * PAGES + (4 * s - PAGES + VR))
                    nc.scalar.copy(pt_s[:, :, :].rearrange("p t q -> p (t q)"), t2_bank(("s", s))).then_inc(act_t2, 1)

                def new_evac(b):
                    act.wait_ge(pe_t2, t2_at(b, ("n", SLOTS - 1)) + 1)
                    nc.scalar.copy(pt_n[:, :], b6[0:TS, 0:P]).then_inc(act_t2, 1)

                def batch(b, sample):
                    for s in range(SLOTS):
                        if sample:
                            sample_exp(b, s)
                        k_evac(b, s, 0, 0)
                        if sample:
                            sample_evac(b, s)
                        prompt_exp(b, s, 0)
                        k_evac(b, s, 0, 2)
                        if sample and s == SLOTS - 1:
                            new_evac(b)
                        k_evac(b, s, 1, 0)
                        prompt_exp(b, s, 1)
                        k_evac(b, s, 1, 2)
                        prompt_evac(b, s, 0)
                        prompt_evac(b, s, 1)

                batch(0, False)
                with act.Fori(1, NB) as b:
                    batch(b, True)

                def final_norm_row(n):
                    rows, src = (TS, xs_c[:, :]) if n == TT - 1 else (P, x1_t[min(n, TT - 1) % 3][:, :])
                    act.wait_ge(dve_y, n + 1)
                    nc.scalar.activation(jk2[0:rows, :], src, ACT.Square, accum_out=ss[0:rows, n:n + 1]).then_inc(act_y, 1)
                    act.wait_ge(dve_v, n + 1)
                    nc.scalar.activation(ss[0:rows, n:n + 1], ss[0:rows, n:n + 1], ACT.Sqrt).then_inc(act_r, 1)

                def high_z(i):
                    past(act, pe_y, i - 1)
                    nc.scalar.copy(z_hi[i % 2][:, :, :], z_t[:, :, P * i:P * i + P]).then_inc(act_zh, 1)

                def high_w(k):
                    act.wait_ge(k_full[k], 64 * NB + 16)
                    nc.scalar.copy(wo_hi[k][:, :], w_o[:, k, :]).then_inc(act_wh, 1)

                sample_exp(NB, 0)
                act.wait_ge(dve_op, NB * SLOTS)
                act.wait_ge(dve_s, NB * 9)
                high_z(0)
                high_w(0)
                for i in range(TT):
                    if i < 4:
                        sample_evac(NB, 2 * i)
                        sample_exp(NB, 2 * i + 1)
                    if i == 0:
                        for k in range(1, KT8):
                            high_w(k)
                    if i >= 1:
                        final_norm_row(i - 1)
                    if i < TT - 1:
                        high_z(i + 1)
                    if i < 4:
                        sample_evac(NB, 2 * i + 1)
                        if i < 3:
                            sample_exp(NB, 2 * i + 2)
                        else:
                            new_evac(NB)
                final_norm_row(TT - 1)
                final_norm_row(TT)

            @attend.vector
            def _(dve):
                V = nc.vector
                N_CA, N_CV = 17, 4

                def k_evac(b, s, h, m):
                    dve.wait_ge(pe_kt, b * 64 + (8 * s + 4 * h + m + 1))
                    past(dve, pe_qk, b * 16 + (2 * s + h - 1))
                    V.tensor_copy(kt[h][:, 2 * m:2 * m + 2, :].rearrange("p a k -> p (a k)"), b5[:, :]).then_inc(dve_kt, 1)

                def prompt_max(b, s, h):
                    dve.wait_ge(pe_s, b * 16 + (2 * s + h + 1))
                    first, last = score_columns(s)
                    V.tensor_reduce(pp_nm[:, h:h + 1], ps_a[:, first:last], AX, ALU.max, negate=True)\
                        .then_inc(dve_mx, 1)

                def prompt_norm(b, s, h):
                    dve.wait_ge(act_p, b * 16 + (2 * s + h + 1))
                    V.reciprocal(pp_r[:, h:h + 1], pp_l[:, h:h + 1]).then_inc(dve_ca, 1)
                    dve.wait_ge(dve_ca, b * N_CA + (2 * s + h + 1))
                    n = P * (QBLOCKS[s] + 1)
                    V.tensor_scalar(p_p[:, h, 0:n], p_p[:, h, 0:n], pp_r[:, h:h + 1], None, ALU.mult).then_inc(dve_pn, 1)

                def queries(b):
                    past(dve, pe_new, b)
                    for par in range(2):
                        for hh in range(2):
                            c = 8 * par + NQ * hh
                            last = V.tensor_copy(q_bd[64 * hh:64 * hh + 64, par::2, c:c + NQ],
                                                 q_s[64 * hh:64 * hh + 64, par::2, bass.ds(b * NQ, NQ)])
                    last.then_inc(dve_q, 1)

                def sample_scores(b, s):
                    dve.wait_ge(pe_qk, b * 16 + (2 * s + 2))
                    if s % 4 == 0:
                        dve.wait_ge(ld_d[s // 4], b * 64 + 64)
                    c = slice(512 * s, 512 * s + 512)
                    V.scalar_tensor_tensor(s_sb[:, c], b7[:, :], cq[:, bass.ds(b, 1)], d_sb[:, c], ALU.add, ALU.add)\
                        .then_inc(dve_s, 1)
                    dve.wait_ge(dve_s, b * 9 + (s + 1))
                    V.tensor_reduce(st_max[:, s:s + 1], s_sb[:, c], AX, ALU.max)

                def new_scores(b):
                    dve.wait_ge(pe_new, b + 1)
                    V.scalar_tensor_tensor(s_sb[:, PAST:PAST + TS], b5[:, 0:TS], cq[:, bass.ds(b, 1)],
                                           d_new[:, bass.ds(b, 1), :].rearrange("p o t -> p (o t)"), ALU.add, ALU.add)\
                        .then_inc(dve_s, 1)
                    dve.wait_ge(dve_s, b * 9 + 9)
                    V.tensor_reduce(st_max[:, 8:9], s_sb[:, PAST:PAST + TS], AX, ALU.max).then_inc(dve_ca, 1)
                    dve.wait_ge(dve_ca, b * N_CA + N_CA)

                def gate(b, s):
                    dve.wait_ge(pe_pvp, b * 16 + (2 * s + 2))
                    r = P * QBLOCKS[s]
                    z = z_t[:, bass.ds(b, 1), r:r + P].rearrange("p o t -> p (o t)")
                    V.tensor_tensor(z, z, ps_b[:, 512:512 + P], ALU.mult).then_inc(dve_op, 1)

                def sum_exp(b):
                    dve.wait_ge(act_e, b * 9)
                    V.tensor_reduce(st_l[:, 0:1], st_sum[:, :], AX, ALU.add).then_inc(dve_cv, 1)

                def sample_out(b):
                    dve.wait_ge(dve_cv, b * N_CV + (1 - N_CV))
                    V.reciprocal(st_l[:, 1:2], st_l[:, 0:1]).then_inc(dve_cv, 1)
                    dve.wait_ge(dve_cv, b * N_CV + (2 - N_CV))
                    V.tensor_scalar(hm_l[:, :], con[:, C_HM:C_HM + 4], st_l[:, 1:2], None, ALU.mult).then_inc(dve_cv, 1)
                    dve.wait_ge(dve_cv, b * N_CV + (3 - N_CV))
                    dve.wait_ge(pe_vo, b)
                    V.tensor_tensor(o_raw[:, :, :], ps_b[:, 0:256].rearrange("p (h d) -> p h d", d=HD),
                                    hm_l[:, :].unsqueeze(2).to_broadcast([P, 4, HD]), ALU.mult).then_inc(dve_cv, 1)
                    dve.wait_ge(dve_cv, b * N_CV)
                    dve.wait_ge(o_free, b)
                    V.tensor_reduce(o_n[:, :], o_raw[:, :, :].rearrange("p h d -> p d h"), AX, ALU.add).then_inc(dve_ov, 1)

                def batch(b, sample):
                    for s in range(SLOTS):
                        k_evac(b, s, 0, 1)
                        if s == 0:
                            prompt_max(b, 0, 0)
                            queries(b)
                        k_evac(b, s, 0, 3)
                        prompt_norm(b, s, 0)
                        prompt_max(b, s, 1)
                        k_evac(b, s, 1, 1)
                        k_evac(b, s, 1, 3)
                        prompt_norm(b, s, 1)
                        if sample and s == SLOTS - 1:
                            sum_exp(b)
                            sample_out(b)
                        sample_scores(b, s)
                        if s < SLOTS - 1:
                            prompt_max(b, s + 1, 0)
                        else:
                            new_scores(b)
                            V.tensor_reduce(st_nm[:, :], st_max[:, :], AX, ALU.max, negate=True).then_inc(dve_nm, 1)
                        gate(b, s)

                dve.sem_inc(dve_ov, 1)
                dve.wait_ge(st_dense, 64)
                V.memset(d_sb[:, :], 0.0).then_inc(dve_d0, 1)
                batch(0, False)
                with dve.Fori(1, NB) as b:
                    batch(b, True)

                def final(n, dst, rows):
                    dve.wait_ge(act_y, n + 1)
                    V.tensor_scalar(ss[0:rows, n:n + 1], ss[0:rows, n:n + 1], 1.0 / DM, EPS, ALU.mult, ALU.add)\
                        .then_inc(dve_v, 1)
                    dve.wait_ge(act_r, n + 1)
                    V.reciprocal(ss[0:rows, n:n + 1], ss[0:rows, n:n + 1]).then_inc(dve_ce, 1)
                    dve.wait_ge(dve_ce, n + 1)
                    V.scalar_tensor_tensor(dst, dst, ss[0:rows, n:n + 1], fn_b[0:rows, :], ALU.mult, ALU.mult)\
                        .then_inc(dve_n, 1)

                def low_z(i):
                    dve.wait_ge(act_zh, i + 1)
                    c = slice(P * i, P * i + P)
                    V.tensor_tensor(z_lo[:, :, c], z_t[:, :, c], z_hi[i % 2][:, :, :].bitcast(F32), ALU.subtract)\
                        .then_inc(dve_zl, 1)

                low_z(0)
                for k in range(KT8):
                    dve.wait_ge(act_wh, k + 1)
                    V.tensor_tensor(wo_lo[:, k, :], w_o[:, k, :], wo_hi[k][:, :].bitcast(F32), ALU.subtract)\
                        .then_inc(dve_wl, 1)
                dve.wait_ge(ld_fn, 16)
                for i in range(TT):
                    if i < TT - 1:
                        low_z(i + 1)
                    if i == 4:
                        sum_exp(NB)
                        sample_out(NB)
                    if i == 5:
                        dve.wait_ge(pe_sm, 1)
                        V.tensor_tensor(h_s[:, :, :], b4[:, 0:KT8 * TS].rearrange("p (k t) -> p k t", t=TS),
                                        z_t[:, :, SEQ:SEQ + TS], ALU.mult).then_inc(dve_sm, 1)
                    if i == 6:
                        dve.wait_ge(pe_sm, 2)
                        V.tensor_copy(xs_c[:, :], x_s[32:64, :])
                        V.tensor_copy(sm_p[:, :], ps_b[:, :]).then_inc(dve_sm, 1)
                        dve.wait_ge(dve_sm, 2)
                        V.tensor_tensor(xs_c[:, :], xs_c[:, :], x_s[0:TS, :], ALU.add).then_inc(dve_sm, 1)
                    if i == 7:
                        dve.wait_ge(dve_sm, 3)
                        dve.wait_ge(pe_sm, 3)
                        V.tensor_tensor(xs_c[:, :], xs_c[:, :], ps_b[0:TS, :], ALU.add).then_inc(dve_y, 1)
                        final(TT - 1, xs_c[:, :], TS)
                    dve.wait_ge(pe_y, i + 1)
                    dve.wait_ge(ld_x1[i % 3], 16 * (i // 3 + 1))
                    V.tensor_tensor(x1_t[i % 3][:, 0:512], x1_t[i % 3][:, 0:512], y_ps[i % 2][0], ALU.add)
                    V.tensor_tensor(x1_t[i % 3][:, 512:DM], x1_t[i % 3][:, 512:DM], y_ps[i % 2][1], ALU.add)\
                        .then_inc(dve_y, 1)
                    final(i if i < TT - 1 else TT, x1_t[i % 3][:, :], P)


_INS = ["x_prompt", "x_sample", "state_pool", "cache_k", "cache_v", "cache_logf", "page_table", "norm_g",
        "w_in_pool", "pool_mix", "pool_scale", "w_out_pool", "w_in_attn", "b_forget", "w_out_attn", "final_norm"]
_OUTS = [(1, SEQ, DM), (NB, NQ, DM), (1, 1, CTX, PW), (1, NB, CTX, PW), (1, 1, SEQ, NH, HD), (1, 1, SEQ, NH, HD),
         (1, 1, SEQ, NH), (1, NB, NQ, NH, HD), (1, NB, NQ, NH, HD), (1, NB, NQ, NH)]


def kernel(**inputs):
    import concourse.bacc as bacc
    from concourse.bass_utils import run_bass_kernel_spmd as run

    nc = bacc.Bacc("TRN2", target_bir_lowering=False, num_devices=1)
    arrays = {f"in_{n}_dram": np.ascontiguousarray(inputs[n]) for n in _INS}
    arrays["in_consts_dram"] = constants()
    args = [nc.dram_tensor(n, a.shape, mybir.dt.from_np(a.dtype), kind="ExternalInput").ap()
            for n, a in arrays.items()]
    args += [nc.dram_tensor(f"out_{i}_dram", shape, F32, kind="ExternalOutput").ap()
             for i, shape in enumerate(_OUTS)]
    build(nc, *args)
    r = run(nc, [arrays], core_ids=[0])
    return tuple(r.results[0][f"out_{i}_dram"] for i in range(len(_OUTS)))
```
